# Optimizing a Trainium2 kernel written in Bass

```python
import math
import jax, jax.numpy as jnp
from jax import lax
import numpy as np

D_MODEL = 1024
BATCH = 1
SEQ = 256
DEPTH = 1

HEAD_DIM = 64
HEADS_PER_GROUP = 4
ATTN_GROUPS = ((128, 1), (512, 4), (2048, 16))
N_ATTN_HEADS = HEADS_PER_GROUP * len(ATTN_GROUPS)
ATTN_WIDTH = N_ATTN_HEADS * HEAD_DIM
KEYS_PER_QUERY = ATTN_GROUPS[0][0] // ATTN_GROUPS[0][1] + 1
MAX_WINDOW = max(w for w, _ in ATTN_GROUPS)
Q_BLOCK = 128
NEG_INF = -1e30
CONV_CH = 512
CONV_WIDTH = 31
N_BRANCHES = 2
IN_COLS = 2 * CONV_CH + 3 * ATTN_WIDTH + N_BRANCHES * D_MODEL
REL_BUCKETS = 32
REL_MAX_DISTANCE = 2048
PEER_HEADS = 8
PEER_N_KEYS = 128
PEER_N_EXPERTS = PEER_N_KEYS * PEER_N_KEYS
PEER_KEY_DIM = 256
PEER_TOPK = 16
TOKEN_CHUNK = 128
EPS = 1e-6

kernel_name = "hybrid_conv_dilattn_peer_block"

def rmsnorm(x, g):
    x32 = x.astype(jnp.float32)
    y = x32 * lax.rsqrt(jnp.mean(x32 * x32, axis=-1, keepdims=True) + EPS)
    return y.astype(x.dtype) * g

def layernorm(x, g, b):
    x32 = x.astype(jnp.float32)
    mu = jnp.mean(x32, axis=-1, keepdims=True)
    var = jnp.mean(jnp.square(x32 - mu), axis=-1, keepdims=True)
    y = (x32 - mu) * lax.rsqrt(var + EPS)
    return y.astype(x.dtype) * g + b

def t5_causal_bucket(distance):
    n = distance.astype(jnp.int32)
    max_exact = REL_BUCKETS // 2
    nf = jnp.maximum(n, 1).astype(jnp.float32)
    large = max_exact + (jnp.log(nf / max_exact) / math.log(REL_MAX_DISTANCE / max_exact)
                         * (REL_BUCKETS - max_exact)).astype(jnp.int32)
    large = jnp.minimum(large, REL_BUCKETS - 1)
    return jnp.where(n < max_exact, n, large)

def conformer_conv(glu_in, b_glu, dw_w, dw_b, ln_g, ln_b, w_proj, b_proj):
    a, gate = jnp.split(glu_in + b_glu, 2, axis=-1)
    u = a * jax.nn.sigmoid(gate)
    u = lax.conv_general_dilated(u, dw_w, window_strides=(1,),
                                 padding=[(CONV_WIDTH - 1, 0)],
                                 dimension_numbers=('NWC', 'WIO', 'NWC'),
                                 feature_group_count=CONV_CH) + dw_b
    u = jax.nn.silu(layernorm(u, ln_g, ln_b))
    return u @ w_proj + b_proj

def dilated_attention(q, k, v, rel_bias):
    B, S = q.shape[0], q.shape[1]
    pad = ((0, 0), (MAX_WINDOW, 0), (0, 0), (0, 0))
    k_pad, v_pad = jnp.pad(k, pad), jnp.pad(v, pad)
    scale = HEAD_DIM ** -0.5
    steps = jnp.arange(KEYS_PER_QUERY)
    offs = jnp.arange(Q_BLOCK)
    k_groups, v_groups, biases = [], [], []
    for g, (w, d) in enumerate(ATTN_GROUPS):
        hs = slice(g * HEADS_PER_GROUP, (g + 1) * HEADS_PER_GROUP)
        k_groups.append(k_pad[:, :, hs])
        v_groups.append(v_pad[:, :, hs])
        biases.append(rel_bias[t5_causal_bucket(steps * d)][:, hs].T)

    def block(blk):
        t0 = blk * Q_BLOCK
        qb = lax.dynamic_slice_in_dim(q, t0, Q_BLOCK, axis=1)
        outs, lses = [], []
        for g, (w, d) in enumerate(ATTN_GROUPS):
            hs = slice(g * HEADS_PER_GROUP, (g + 1) * HEADS_PER_GROUP)
            pos = t0 + offs[:, None] - d * steps[None, :]
            valid = pos >= 0
            idx = pos + MAX_WINDOW
            kg = jnp.take(k_groups[g], idx, axis=1)
            vg = jnp.take(v_groups[g], idx, axis=1)
            s = jnp.einsum('bqhd,bqkhd->bhqk', qb[:, :, hs], kg).astype(jnp.float32) * scale
            s = s + biases[g][None, :, None, :].astype(jnp.float32)
            s = jnp.where(valid[None, None], s, NEG_INF)
            lse = jax.nn.logsumexp(s, axis=-1, keepdims=True)
            p = jnp.exp(s - lse).astype(v.dtype)
            outs.append(jnp.einsum('bhqk,bqkhd->bqhd', p, vg))
            lses.append(lse[..., 0])
        wgt = jax.nn.softmax(jnp.stack(lses, axis=0), axis=0)
        wgt = jnp.transpose(wgt, (0, 1, 3, 2))[..., None].astype(v.dtype)
        o = jnp.concatenate([outs[g] * wgt[g] for g in range(len(ATTN_GROUPS))], axis=2)
        return o.reshape(B, Q_BLOCK, ATTN_WIDTH)

    o = lax.map(block, jnp.arange(S // Q_BLOCK))
    return jnp.transpose(o, (1, 0, 2, 3)).reshape(B, S, ATTN_WIDTH)

def hybrid_mixer(xn, w_in, conv_b_glu, conv_dw_w, conv_dw_b, conv_ln_g, conv_ln_b,
                 conv_w_proj, conv_b_proj, q_norm_g, k_norm_g, rel_bias, attn_w_proj, mix_w_out):
    B, S, _ = xn.shape
    proj = xn @ w_in
    c0 = 2 * CONV_CH
    glu_in, q, k, v, gates = jnp.split(
        proj, [c0, c0 + ATTN_WIDTH, c0 + 2 * ATTN_WIDTH, c0 + 3 * ATTN_WIDTH], axis=-1)
    conv_out = conformer_conv(glu_in, conv_b_glu, conv_dw_w, conv_dw_b,
                              conv_ln_g, conv_ln_b, conv_w_proj, conv_b_proj)
    heads = (B, S, N_ATTN_HEADS, HEAD_DIM)
    q = rmsnorm(q.reshape(heads), q_norm_g)
    k = rmsnorm(k.reshape(heads), k_norm_g)
    v = v.reshape(heads)
    attn_out = dilated_attention(q, k, v, rel_bias) @ attn_w_proj
    g_conv, g_attn = jnp.split(gates, 2, axis=-1)
    merged = jax.nn.sigmoid(g_conv) * conv_out + jax.nn.sigmoid(g_attn) * attn_out
    return merged @ mix_w_out

def peer(xn, w_q, sub_keys, u_tab, v_tab):
    B, S, D = xn.shape
    half = PEER_KEY_DIM // 2

    def chunk(xc):
        q = (xc @ w_q).reshape(TOKEN_CHUNK, PEER_HEADS, 2, half)
        s = jnp.einsum('thpd,hpnd->thpn', q, sub_keys).astype(jnp.float32)
        top_s, top_i = lax.top_k(s, PEER_TOPK)
        cand = top_s[:, :, 0, :, None] + top_s[:, :, 1, None, :]
        best_s, best_c = lax.top_k(cand.reshape(TOKEN_CHUNK, PEER_HEADS, PEER_TOPK * PEER_TOPK), PEER_TOPK)
        i1 = jnp.take_along_axis(top_i[:, :, 0], best_c // PEER_TOPK, axis=-1)
        i2 = jnp.take_along_axis(top_i[:, :, 1], best_c % PEER_TOPK, axis=-1)
        e = i1 * PEER_N_KEYS + i2
        gate = jax.nn.softmax(best_s, axis=-1).astype(xc.dtype)
        h = jnp.einsum('thkd,td->thk', u_tab[e], xc)
        act = jax.nn.gelu(h, approximate=False) * gate
        return jnp.einsum('thk,thkd->td', act, v_tab[e])

    y = lax.map(chunk, xn.reshape(-1, TOKEN_CHUNK, D))
    return y.reshape(B, S, D)

def setup_inputs(seed: int = 0) -> dict:
    key = jax.random.key(seed)
    ks = jax.random.split(key, 20)
    f32 = jnp.float32
    nrm = lambda k, shape, s: jax.random.normal(k, shape, f32) * s
    L, D = DEPTH, D_MODEL
    return {
        "x": nrm(ks[0], (BATCH, SEQ, D), 1.0),
        "w_in": nrm(ks[1], (L, D, IN_COLS), D ** -0.5),
        "conv_b_glu": nrm(ks[2], (L, 2 * CONV_CH), 0.02),
        "conv_dw_w": nrm(ks[3], (L, CONV_WIDTH, 1, CONV_CH), CONV_WIDTH ** -0.5),
        "conv_dw_b": nrm(ks[4], (L, CONV_CH), 0.02),
        "conv_ln_g": 1.0 + nrm(ks[5], (L, CONV_CH), 0.02),
        "conv_ln_b": nrm(ks[6], (L, CONV_CH), 0.02),
        "conv_w_proj": nrm(ks[7], (L, CONV_CH, D), CONV_CH ** -0.5),
        "conv_b_proj": nrm(ks[8], (L, D), 0.02),
        "q_norm_g": 1.0 + nrm(ks[9], (L, HEAD_DIM), 0.02),
        "k_norm_g": 1.0 + nrm(ks[10], (L, HEAD_DIM), 0.02),
        "rel_bias": nrm(ks[11], (REL_BUCKETS, N_ATTN_HEADS), 0.5),
        "attn_w_proj": nrm(ks[12], (L, ATTN_WIDTH, D), ATTN_WIDTH ** -0.5),
        "mix_w_out": nrm(ks[13], (L, D, D), D ** -0.5),
        "norm1_g": 1.0 + nrm(ks[14], (L, D), 0.02),
        "norm2_g": 1.0 + nrm(ks[15], (L, D), 0.02),
        "peer_w_q": nrm(ks[16], (L, D, PEER_HEADS * PEER_KEY_DIM), D ** -0.5),
        "peer_sub_keys": nrm(ks[17], (L, PEER_HEADS, 2, PEER_N_KEYS, PEER_KEY_DIM // 2), (PEER_KEY_DIM // 2) ** -0.5),
        "peer_u": nrm(ks[18], (L, PEER_N_EXPERTS, D), D ** -0.5),
        "peer_v": nrm(ks[19], (L, PEER_N_EXPERTS, D), 0.5),
    }

def reference(x, w_in, conv_b_glu, conv_dw_w, conv_dw_b, conv_ln_g, conv_ln_b, conv_w_proj,
              conv_b_proj, q_norm_g, k_norm_g, rel_bias, attn_w_proj, mix_w_out, norm1_g,
              norm2_g, peer_w_q, peer_sub_keys, peer_u, peer_v):
    for l in range(DEPTH):
        xn = rmsnorm(x, norm1_g[l])
        x = x + hybrid_mixer(xn, w_in[l], conv_b_glu[l], conv_dw_w[l], conv_dw_b[l],
                             conv_ln_g[l], conv_ln_b[l], conv_w_proj[l], conv_b_proj[l],
                             q_norm_g[l], k_norm_g[l], rel_bias, attn_w_proj[l], mix_w_out[l])
        hn = rmsnorm(x, norm2_g[l])
        x = x + peer(hn, peer_w_q[l], peer_sub_keys[l], peer_u[l], peer_v[l])
    return x


_drawn_inputs = setup_inputs


def setup_inputs(seed=0):
    import zlib

    import numpy as np

    out = dict(_drawn_inputs(seed))
    spreads = {}
    factors = {'q_norm_g': 5.217, 'k_norm_g': 6.511}
    for name, (base, spread) in spreads.items():
        noise = np.random.default_rng([zlib.crc32(name.encode()), seed]).standard_normal(out[name].shape)
        drawn = base * np.exp(spread * noise) if base else spread * noise
        out[name] = __import__('jax').numpy.asarray(drawn.astype(out[name].dtype))
    for name, factor in factors.items():
        out[name] = (out[name] * factor).astype(out[name].dtype)
    return out
```

```python
from contextlib import ExitStack

import numpy as np

import concourse.bass as bass
from concourse import mybir

F32 = mybir.dt.float32
F32R = mybir.dt.float32r
U32 = mybir.dt.uint32
BF16 = mybir.dt.bfloat16
ALU = mybir.AluOpType
ACT = mybir.ActivationFunctionType
AX = mybir.AxisListType

P = 128
D = 1024
T = 256
KB = D // P
TC = T // P
CONV_CH, TAPS = 512, 31
CB = CONV_CH // P
HEADS, HD = 12, 64
SLOTS, GROUPS = 4, 3
AW = HEADS * HD
AB = AW // P
WINDOWS = ((128, 1), (512, 4), (2048, 16))
BUCKETS, MAX_DISTANCE = 32, 2048
PH, NK, TOPK = 8, 128, 16
HALVES = 2 * PH
EPS = 1e-6
NEG = -1e30
LOWEST = -3.0e38
BW = 384

T_GLU, T_QK, T_V, T_GATE = 0, 8, 20, 26
T_CONV, T_ATT, T_MIX, T_WQ = 42, 46, 52, 60
N_FRONT = 76
N_U = N_V = NK
RING = 4
LEAD = 3
HALF = NK // 2
TOK = 4


def jobs_in_order():
    order = [(("ssq1",), None)] + [(("bias", h), None) for h in range(HEADS)]
    for n in range(T_CONV):
        if n < T_QK:
            order.append((("glu", n), n))
        elif n < T_V:
            order.append((("qk", n - T_QK), n))
        elif n < T_GATE:
            order.append((("v", n - T_V), n))
        else:
            order.append((("gate", n - T_GATE), n))
        if n >= T_QK + 3 and (n - T_QK - 3) % 2 == 0 and (n - T_QK - 3) // 2 < AB:
            order.append((("qkssq", (n - T_QK - 3) // 2), None))
        if n >= T_V + 2 and n % 2 == 0 and n <= T_V + AB:
            order.append((("vt", (n - T_V - 2) // 2), None))
        if 33 <= n < 39:
            order += [(("score", 2 * (n - 33)), None), (("score", 2 * (n - 33) + 1), None)]
        if n == 39:
            order.append((("lnsum",), None))
        if n == 41:
            order.append((("lnvar",), None))
    for b in range(AB):
        order += [(("pT", 2 * b), None), (("pT", 2 * b + 1), None)]
        if b:
            order.append((("o", b - 1), None))
    order.append((("o", AB - 1), None))
    for n in range(CB):
        order += [(("conv", 2 * n), None), (("conv", 2 * n + 1), T_CONV + n)]
    for b in range(KB):
        for u in range(AB * b, AB * b + AB):
            if u % 8 == 7 and u != AB * b + AB - 1:
                order.append((None, T_ATT + u // 8))
        last = AB * b + AB - 1
        order.append((("attn", b), T_ATT + last // 8 if last % 8 == 7 else None))
    order += [(("mix", b), T_MIX + b) for b in range(KB)]
    order.append((("ssq2",), None))
    order += [(("wq", u), T_WQ + u) for u in range(HALVES)]
    return order


ORDER = jobs_in_order()
STEP_OF_JOB = {job: i + 1 for i, (job, _) in enumerate(ORDER) if job}
STEP_OF_TILE = {tile: i + 1 for i, (_, tile) in enumerate(ORDER) if tile is not None}
FRONT_STEPS = len(ORDER)
N_SC = 2 * HALVES // 4
JOBS = [job for job, _ in ORDER if job] + [("sc", j) for j in range(N_SC)]
BANK_OF = {job: i % 8 for i, job in enumerate(JOBS)}
BY_DVE = ("score", "lnsum", "o", "conv", "attn", "mix")


def freed_by_dve(job):
    return job[0] in BY_DVE or (job[0] == "glu" and job[1] % 2 == 1)


FREED = {}
_n = {True: 0, False: 0}
for _job in JOBS:
    _n[freed_by_dve(_job)] += 1
    FREED[_job] = _n[freed_by_dve(_job)]

PAIRS = [(0, 2), (1, 3), (4, 6), (5, 7), (8, 10), (9, 11)]

C_N1, C_N2, C_GLU, C_DW, C_DWB = 0, 8, 16, 24, 24 + CB * TAPS
C_LNG = C_DWB + CB
C_LNB = C_LNG + CB
C_BP = C_LNB + CB
C_QG = C_BP + KB
C_KG = C_QG + 1
N_COLS = C_KG + 1


def hybrid_block(nc, x_t, front, cols, rel_bias, onehot, sub_keys, u_tiles, v_tiles, out):
    toeplitz = nc.dram_tensor("toeplitz", (HEADS, P * BW), F32, kind="Internal").ap()
    with ExitStack() as ctx:
        def sb(name, shape, dt=F32, stack=ctx):
            return stack.enter_context(nc.sbuf_tensor(name, shape, dt))

        def sem(name):
            return ctx.enter_context(nc.semaphore(name))

        bank = [ctx.enter_context(nc.psum_tensor(f"bank{i}", [P, 512], F32)) for i in range(8)]

        raw = sb("raw", [P, RING, D])
        hi = sb("hi", [P, RING, D], F32R)
        lo = sb("lo", [P, RING, D], F32R)
        nrm_hi = sb("nrm_hi", [P, KB, T], F32R)
        nrm_lo = sb("nrm_lo", [P, KB, T], F32R)
        ident = sb("ident", [P, P])
        iota = sb("iota", [P, TOPK])
        inner = ExitStack()

        def tmp(name, shape, dt=F32):
            return sb(name, shape, dt, inner)

        ones = tmp("ones", [P, P])
        bones = tmp("bones", [P, P])
        prm = tmp("prm", [P, N_COLS])
        relx = tmp("relx", [BUCKETS + 1, HEADS])
        relb = tmp("relb", [BUCKETS + 1, HEADS, P])
        oneh = tmp("oneh", [BUCKETS + 1, GROUPS, BW])
        sq = tmp("sq", [P, KB, T])
        rs = tmp("rs", [P, 2, 512])
        u_pad = tmp("u_pad", [P, CB, TAPS - 1 + T])
        sig = tmp("sig", [P, CB, T])
        acc = tmp("acc", [P, CB, T])
        cu_hi = tmp("cu_hi", [P, CB, T], F32R)
        cu_lo = tmp("cu_lo", [P, CB, T], F32R)
        qk = tmp("qk", [P, 2 * AB, T])
        v = tmp("v", [P, TC, AW])
        vT = sig
        gsig = tmp("gsig", [P, 2 * KB, T])
        bias = tmp("bias", [P, HEADS, T])
        prob = tmp("prob", [P, HEADS * BW])
        pT = tmp("pT", [P, 4, 3, P])
        o_hi = tmp("o_hi", [P, AB, T], F32R)
        o_lo = tmp("o_lo", [P, AB, T], F32R)
        stat = tmp("stat", [P, 16, TC * HEADS])
        resid = tmp("resid", [P, KB, T])
        inner.close()
        act = sb("act", [P, NK, T])
        iota4 = sb("iota4", [P, NK, TOK], BF16)
        keys = sb("keys", [P, 2, T], BF16)
        parts = sb("parts", [P, 3, T], BF16)
        ohA = sb("ohA", [P, 2, NK, TOK], BF16)
        eqB = sb("eqB", [P, 2, HALF, TOK], BF16)
        ohB = sb("ohB", [P, 2, 3, HALF, TOK], BF16)

        p3 = prob[:, :].rearrange("p (h n) -> p h n", n=BW)
        qT = prob[:, 0:HALVES * T].rearrange("p (u t) -> p u t", t=T)
        skT = qk[:, 0:HALVES // 2, :].rearrange("p a t -> p (a t)").rearrange("p (u n) -> p u n", n=NK)
        negm, lsum, lnl, lse, ew, zz, fac = [stat[:, i, :] for i in range(7)]
        gmax, gsum = stat[:, 7, 0:TC * SLOTS], stat[:, 8, 0:TC * SLOTS]
        def part(t0, n):
            return act[:, t0:t0 + n, :].rearrange("p a t -> p (a t)")

        S = part(112, 16).rearrange("p (u n) -> p u n", n=NK)
        cand = part(104, 8).rearrange("p (h n) -> p h n", n=TOPK * TOPK)
        eq = part(96, 8)
        topv = part(64, 2).rearrange("p (u k) -> p u k", k=TOPK)
        topi = part(66, 2).bitcast(U32).rearrange("p (u k) -> p u k", k=TOPK)
        topf = part(68, 2).rearrange("p (u k) -> p u k", k=TOPK)
        bestv = part(70, 1).rearrange("p (u k) -> p u k", k=TOPK)
        besti = part(71, 1).bitcast(U32)
        bc1 = part(72, 1).bitcast(U32)
        bc2 = part(73, 1).bitcast(U32)
        cf1 = part(74, 1)
        cf2 = part(75, 1)
        sel = part(76, 2).rearrange("p (w c n) -> p w c n", w=2, c=TC)
        ex = part(78, 1)
        gate = part(79, 1).rearrange("p (c n) -> p c n", c=TC)
        pickf = part(81, 4).rearrange("p (a t) -> p a t", a=4)
        zs = part(80, 1)[:, 0:3 * TC * PH].rearrange("p (a n) -> p a n", a=3)
        yout = part(0, 8)

        raw_in = [sem(f"raw_in{i}") for i in range(RING)]
        x_in, prm_in, rel_in, bias_out, bias_in, sk_in, y_out = [sem(s) for s in (
            "x_in", "prm_in", "rel_in", "bias_out", "bias_in", "sk_in", "y_out")]
        hi_ready, lo_pool, lo_dve = sem("hi_ready"), sem("lo_pool"), sem("lo_dve")
        pe_step = sem("pe_step")
        act_evac, dve_evac = sem("act_evac"), sem("dve_evac")
        const = sem("const")
        squared = sem("squared")
        normed = sem("normed")
        nhi, nlo = sem("nhi"), sem("nlo")
        relb_ready = sem("relb_ready")
        sig_ready = sem("sig_ready")
        qk_sq = sem("qk_sq")
        qk_normed = sem("qk_normed")
        tap = sem("tap")
        score_max, exps, lns, wexp, scaled = sem("score_max"), sem("exps"), sem("lns"), sem("wexp"), sem("scaled")
        o_hi_ready = sem("o_hi_ready")
        centred, centred_sq, ln_out, silu, cu_h, cu_l = [sem(s) for s in (
            "centred", "centred_sq", "ln_out", "silu", "cu_h", "cu_l")]
        gates_ready = sem("gates_ready")
        merged, m_hi, m_lo = sem("merged"), sem("m_hi"), sem("m_lo")
        chain = sem("chain")
        sc_ready = sem("sc_ready")
        gelu_done = sem("gelu_done")
        top_done, gexp, gate_ready, pick_T, pick_ready = [sem(s) for s in (
            "top_done", "gexp", "gate_ready", "pick_T", "pick_ready")]
        second, spread, gate_mm, gated = sem("second"), sem("spread"), sem("gate_mm"), sem("gated")
        a_hi, a_lo = sem("a_hi"), sem("a_lo")
        y_began = sem("y_began")
        y_dve, y_act = sem("y_dve"), sem("y_act")

        def wait(eng, s, value):
            if not isinstance(value, int) or value > 0:
                eng.wait_ge(s, value)

        def freed(eng, job):
            wait(eng, dve_evac if freed_by_dve(job) else act_evac, FREED[job])

        def job_done(eng, job):
            eng.wait_ge(pe_step, STEP_OF_JOB[job])

        def step_of(base, it, j):
            if isinstance(it, int) and base + 4 * it + j < N_FRONT:
                return STEP_OF_TILE[base + 4 * it + j]
            return it * 4 + (FRONT_STEPS + base + j - N_FRONT + 1)

        def slot_of(base, j):
            return (base + j) % RING

        def uses(base, it, j):
            return it + ((base + j) // RING + 1)

        def wait_raw(eng, base, it, j):
            eng.wait_ge(raw_in[slot_of(base, j)], uses(base, it, j) * 16)

        def split_hi(act_e, base, it, j):
            s = slot_of(base, j)
            wait_raw(act_e, base, it, j)
            if not (isinstance(it, int) and base + 4 * it + j < RING):
                wait(act_e, pe_step, step_of(base - 4, it, j))
            act_e.copy(hi[:, s, :], raw[:, s, :]).then_inc(hi_ready, 1)

        def by_dve(base, j):
            return slot_of(base, j) == 3

        def lo_count(base, it, j):
            if by_dve(base, j):
                return uses(base, it, j)
            return it * 3 + (3 * ((base + j) // RING) + slot_of(base, j) + 1)

        def wait_lo(eng, base, it, j):
            wait(eng, lo_dve if by_dve(base, j) else lo_pool, lo_count(base, it, j))

        def split_lo(eng, base, it, j):
            s = slot_of(base, j)
            eng.wait_ge(hi_ready, it * 4 + (base + j + 1))
            eng.tensor_tensor(lo[:, s, :], raw[:, s, :], hi[:, s, :].bitcast(F32), ALU.subtract)\
               .then_inc(lo_dve if by_dve(base, j) else lo_pool, 1)

        U0, V0 = N_FRONT, N_FRONT + N_U
        S_U, S_V = FRONT_STEPS, FRONT_STEPS + N_U

        block = ctx.enter_context(nc.Block())

        @block.sync
        def _(sp):
            sp.dma_start(resid[:, :, :], x_t).then_inc(x_in, 16)
            sp.dma_start(prm[:, :], cols).then_inc(prm_in, 16)
            sp.dma_start(oneh[:, :, :], onehot).then_inc(rel_in, 16)
            sp.dma_start(relx[0:BUCKETS, :], rel_bias).then_inc(rel_in, 16)

            def load(src, base, it, j):
                if not (isinstance(it, int) and base + 4 * it + j < RING):
                    wait_lo(sp, base - 4, it, j)
                sp.dma_start(raw[:, slot_of(base, j), :], src).then_inc(raw_in[slot_of(base, j)], 16)

            for g in range(N_FRONT):
                load(front[g], g, 0, 0)
                if g == T_MIX:
                    freed(sp, ("score", 11))
                    sp.dma_start(skT, sub_keys).then_inc(sk_in, 16)
            with sp.Fori(0, N_U // RING) as it:
                for j in range(RING):
                    load(u_tiles[it * RING + j], U0, it, j)
            with sp.Fori(0, N_V // RING) as it:
                for j in range(RING):
                    load(v_tiles[it * RING + j], V0, it, j)
            sp.wait_ge(y_dve, 2)
            sp.wait_ge(y_act, 2)
            for c in range(TC):
                sp.dma_start(out[c], yout[:, c * D:(c + 1) * D]).then_inc(y_out, 16)
            sp.wait_ge(y_out, 16 * TC)

        @block.gpsimd
        def _(pool):
            pool.memset(relx[BUCKETS:BUCKETS + 1, :], NEG).then_inc(const, 1)
            pool.wait_ge(const, 1)
            pool.memset(ones[:, :], 1.0).then_inc(const, 1)
            pool.memset(bones[:, :], 0.0).then_inc(const, 1)
            pool.memset(ident[:, :], 0.0).then_inc(const, 1)
            pool.memset(u_pad[:, :, 0:TAPS - 1], 0.0).then_inc(const, 1)
            pool.wait_ge(const, 5)
            for r in range(2):
                pool.memset(bones[r * HD:(r + 1) * HD, r * HD:(r + 1) * HD], 1.0).then_inc(const, 1)
                pool.wait_ge(const, 6 + r)
            pool.affine_select(out=ident[:, :], in_=ident[:, :], compare_op=ALU.not_equal, fill=1.0,
                               base=0, pattern=[[-1, P]], channel_multiplier=1).then_inc(const, 1)
            pool.iota(iota[:, :], pattern=[[1, TOPK]], base=0, channel_multiplier=0,
                      allow_small_or_imprecise_dtypes=True).then_inc(const, 1)

            def lo_of(g):
                if not by_dve(g, 0):
                    split_lo(pool, g, 0, 0)

            for g in range(6):
                lo_of(g)
            freed(pool, ("bias", HEADS - 1))
            for h in range(HEADS):
                pool.dma_start(toeplitz[h].rearrange("(p w) -> p w", w=BW), p3[:, h, :]).then_inc(bias_out, 16)
            for g in range(6, 12):
                lo_of(g)
            pool.wait_ge(bias_out, 16 * HEADS)
            for h in range(HEADS):
                pool.dma_start(bias[:, h, :], toeplitz[h, P - 1:P - 1 + P * (BW - 1)].rearrange(
                    "(p w) -> p w", w=BW - 1)[:, 0:T]).then_inc(bias_in, 16)
            for g in range(12, N_FRONT + LEAD):
                lo_of(g)
            pool.wait_ge(y_began, 1)
            pool.iota(iota4[:, :, :], pattern=[[1, NK], [0, TOK]], base=0, channel_multiplier=0,
                      allow_small_or_imprecise_dtypes=True).then_inc(const, 1)
            with pool.Fori(0, (N_U + N_V - RING) // RING) as it:
                for j in range(RING):
                    if not by_dve(U0 + LEAD, j):
                        split_lo(pool, U0 + LEAD, it, j)

        @block.scalar
        def _(a):
            a.wait_ge(x_in, 16)
            for r in range(2):
                a.activation(sq[:, 4 * r:4 * r + 4, :], resid[:, 4 * r:4 * r + 4, :], ACT.Square)\
                 .then_inc(squared, 1)
            for g in range(LEAD):
                split_hi(a, g, 0, 0)
            job_done(a, ("ssq1",))
            a.activation(rs[:, 0, 0:T], bank[BANK_OF[("ssq1",)]][:, 0:T], ACT.Sqrt, bias=EPS, scale=1.0 / D)\
             .then_inc(act_evac, 1)
            for r in range(2):
                a.wait_ge(normed, 4 * r + 4)
                a.copy(nrm_hi[:, 4 * r:4 * r + 4, :], sq[:, 4 * r:4 * r + 4, :]).then_inc(nhi, 1)
            for h in range(HEADS):
                job_done(a, ("bias", h))
                a.copy(p3[:, h, :], bank[BANK_OF[("bias", h)]][:, 0:BW]).then_inc(act_evac, 1)

            def exp_of(s):
                c, pair = divmod(s, len(PAIRS))
                w = P * (c + 1)
                a.wait_ge(score_max, s + 1)
                for h in PAIRS[pair]:
                    pr = p3[:, h, c * P:c * P + w]
                    col = c * HEADS + h
                    a.activation(pr, pr, ACT.Exp, bias=negm[:, col:col + 1],
                                 accum_out=lsum[:, col:col + 1]).then_inc(exps, 1)

            def evac_front(n):
                if n < T_QK:
                    if n % 2 == 0:
                        b = n // 2
                        job_done(a, ("glu", n))
                        a.activation(sig[:, b, :], bank[BANK_OF[("glu", n)]][:, 0:T], ACT.Sigmoid,
                                     bias=prm[:, C_GLU + CB + b:C_GLU + CB + b + 1]).then_inc(act_evac, 1)
                elif n < T_V:
                    i = n - T_QK
                    job_done(a, ("qk", i))
                    b = bank[BANK_OF[("qk", i)]][:, 0:T]
                    if i >= KB:
                        job_done(a, ("qkssq", (i - KB) // 2))
                    elif i == 0:
                        a.wait_ge(nhi, 2)
                        a.wait_ge(nlo, 2)
                    a.activation(sq[:, i % KB, :], b, ACT.Square).then_inc(qk_sq, 1)
                    a.copy(qk[:, i, :], b).then_inc(act_evac, 1)
                elif n >= T_GATE:
                    i = n - T_GATE
                    job_done(a, ("gate", i))
                    a.copy(gsig[:, i, :], bank[BANK_OF[("gate", i)]][:, 0:T]).then_inc(act_evac, 1)
                if T_V <= n < T_GATE:
                    i = n - T_V
                    job_done(a, ("v", i))
                    if i == 0:
                        freed(a, ("glu", 2 * CB - 1))
                    if i >= CB:
                        job_done(a, ("vt", (i - CB) // 2))
                    a.copy(vT[:, i % CB, :], bank[BANK_OF[("v", i)]][:, 0:T]).then_inc(act_evac, 1)
                if n >= T_V + 2 and n % 2 == 0 and n <= T_V + AB:
                    i = (n - T_V - 2) // 2
                    job_done(a, ("vt", i))
                    a.copy(v[:, :, 2 * i * P:(2 * i + 2) * P].rearrange("p c (b n) -> p b c n", b=2),
                           bank[BANK_OF[("vt", i)]][:, :].rearrange("p (b c n) -> p b c n", b=2, c=TC))\
                     .then_inc(act_evac, 1)
                if n >= T_QK + 3 and (n - T_QK - 3) % 2 == 0 and (n - T_QK - 3) // 2 < AB:
                    gi = (n - T_QK - 3) // 2
                    job_done(a, ("qkssq", gi))
                    wait(a, qk_normed, gi - 1)
                    a.activation(rs[:, gi % 2, :], bank[BANK_OF[("qkssq", gi)]][:, :], ACT.Sqrt, bias=EPS,
                                 scale=1.0 / HD).then_inc(act_evac, 1)

            for n in range(T_CONV):
                split_hi(a, n + LEAD, 0, 0)
                evac_front(n)
                if n >= 35 and 2 * (n - 35) < 12:
                    exp_of(2 * (n - 35))
                    exp_of(2 * (n - 35) + 1)
            a.wait_ge(centred, 1)
            a.activation(sq[:, 0:CB, :], u_pad[:, :, 0:T], ACT.Square).then_inc(centred_sq, 1)
            a.wait_ge(exps, TC * HEADS)
            a.activation(lnl[:, :], lsum[:, :], ACT.Ln).then_inc(lns, 1)
            a.wait_ge(wexp, TC)
            a.activation(ew[:, :], lse[:, :], ACT.Exp).then_inc(lns, 1)
            job_done(a, ("lnvar",))
            a.wait_ge(qk_normed, AB)
            a.activation(rs[:, 0, 0:T], bank[BANK_OF[("lnvar",)]][:, 0:T], ACT.Sqrt, bias=EPS,
                         scale=1.0 / CONV_CH).then_inc(act_evac, 1)
            a.wait_ge(ln_out, 1)
            for b in range(CB):
                a.activation(acc[:, b, :], acc[:, b, :], ACT.Silu, bias=prm[:, C_LNB + b:C_LNB + b + 1],
                             scale=prm[:, C_LNG + b:C_LNG + b + 1]).then_inc(silu, 1)
            a.wait_ge(silu, CB)
            a.copy(cu_hi[:, :, :], acc[:, :, :]).then_inc(cu_h, 1)
            freed(a, ("gate", 2 * KB - 1))
            for r in range(2):
                a.activation(gsig[:, r * KB:(r + 1) * KB, :], gsig[:, r * KB:(r + 1) * KB, :], ACT.Sigmoid)\
                 .then_inc(gates_ready, 1)

            def copy_pT(h):
                job_done(a, ("pT", h))
                if h >= 4:
                    job_done(a, ("o", (h - 4) // 2))
                a.copy(pT[:, h % 4, :, :], bank[BANK_OF[("pT", h)]][:, 0:3 * P].rearrange(
                    "p (a n) -> p a n", a=3)).then_inc(act_evac, 1)

            def copy_o(b):
                job_done(a, ("o", b))
                a.copy(o_hi[:, b, :], bank[BANK_OF[("o", b)]][:, 0:T]).then_inc(o_hi_ready, 1)

            for b in range(AB):
                copy_pT(2 * b)
                copy_pT(2 * b + 1)
                if b:
                    copy_o(b - 1)
            copy_o(AB - 1)
            for n in range(T_CONV, T_ATT):
                split_hi(a, n + LEAD, 0, 0)
            for b in range(KB):
                if T_ATT + b < T_MIX:
                    split_hi(a, T_ATT + b + LEAD, 0, 0)
                a.wait_ge(merged, b + 1)
                if b == 0:
                    job_done(a, ("gate", 2 * KB - 1))
                a.copy(nrm_hi[:, b, :], gsig[:, b, :]).then_inc(m_hi, 1)
            for b in range(KB):
                split_hi(a, T_MIX + b + LEAD, 0, 0)
                freed(a, ("mix", b))
                a.activation(sq[:, b, :], resid[:, b, :], ACT.Square).then_inc(squared, 1)
            job_done(a, ("ssq2",))
            a.activation(rs[:, 0, 0:T], bank[BANK_OF[("ssq2",)]][:, 0:T], ACT.Sqrt, bias=EPS, scale=1.0 / D)\
             .then_inc(act_evac, 1)
            for r in range(2):
                a.wait_ge(normed, KB + 4 * r + 4)
                a.copy(nrm_hi[:, 4 * r:4 * r + 4, :], sq[:, 4 * r:4 * r + 4, :]).then_inc(nhi, 1)
            for u in range(HALVES):
                split_hi(a, T_WQ + u + LEAD, 0, 0)
                job_done(a, ("wq", u))
                a.copy(qT[:, u, :], bank[BANK_OF[("wq", u)]][:, 0:T]).then_inc(act_evac, 1)
            for j in range(N_SC):
                a.wait_ge(sc_ready, j + 1)
                a.copy(S[:, 4 * j:4 * j + 4, :], bank[BANK_OF[("sc", j)]][:, :].rearrange(
                    "p (u n) -> p u n", n=NK)).then_inc(act_evac, 1)

            def gelu(base_i, it, j):
                a.wait_ge(pe_step, it * 4 + (S_U + base_i + j + 1))
                a.activation(act[:, it * 4 + (base_i + j), :], bank[4 + j % 2][:, 0:T], ACT.Gelu).then_inc(gelu_done, 1)

            a.preload_act_table(ACT.Gelu)
            with a.Fori(0, (HALF - RING) // RING) as it:
                for j in range(RING):
                    split_hi(a, U0 + LEAD, it, j)
                    gelu(0, it, j)
            a.wait_ge(top_done, 1)
            a.activation(ex[:, :], ex[:, :], ACT.Exp).then_inc(gexp, 1)
            for j in range(RING):
                split_hi(a, U0 + HALF - RING + LEAD, 0, j)
                gelu(HALF - RING, 0, j)
            a.wait_ge(pick_ready, 2)
            a.preload_act_table(ACT.Gelu)
            with a.Fori(0, HALF // RING) as it:
                for j in range(RING):
                    split_hi(a, U0 + HALF + LEAD, it, j)
                    gelu(HALF, it, j)

            def a_split(base_i, it, j):
                wait(a, pe_step, it * 4 + (S_V + base_i + j - 3))
                a.copy(nrm_hi[:, (base_i + j) % RING, :], act[:, it * 4 + (base_i + j), :]).then_inc(a_hi, 1)

            a.wait_ge(pe_step, S_V)
            for half in range(2):
                a.wait_ge(gated, HALF * (half + 1))
                a_split(HALF * half, 0, 0)
                with a.Fori(0, HALF // RING - 1) as it:
                    for j in range(RING):
                        a_split(HALF * half + 1, it, j)
                        split_hi(a, V0 + HALF * half + LEAD, it, j)
                for j in range(RING):
                    if j < RING - 1:
                        a_split(HALF * (half + 1) - RING + 1, 0, j)
                    if half == 0 or j == 0:
                        split_hi(a, V0 + HALF * (half + 1) - RING + LEAD, 0, j)
            a.wait_ge(pe_step, S_V + N_V)
            for half in range(2):
                a.copy(yout[:, D + 512 * half:D + 512 * half + 512], bank[2 + half][:, :]).then_inc(y_act, 1)

        @block.vector
        def _(dve):
            links = [0]

            def link(ins):
                links[0] += 1
                ins.then_inc(chain, 1)
                dve.wait_ge(chain, links[0])

            def lo_of(g):
                if by_dve(g, 0):
                    split_lo(dve, g, 0, 0)

            def normalise(gain, round_):
                link(dve.reciprocal(rs[:, 0, 0:T], rs[:, 0, 0:T]))
                for k in range(KB):
                    dve.scalar_tensor_tensor(out=sq[:, k, :], in0=resid[:, k, :], scalar=prm[:, gain + k:gain + k + 1],
                                             in1=rs[:, 0, 0:T], op0=ALU.mult, op1=ALU.mult).then_inc(normed, 1)
                dve.wait_ge(normed, KB * (round_ + 1))
                for r in range(2):
                    dve.wait_ge(nhi, 2 * round_ + r + 1)
                    dve.tensor_tensor(nrm_lo[:, 4 * r:4 * r + 4, :], sq[:, 4 * r:4 * r + 4, :],
                                      nrm_hi[:, 4 * r:4 * r + 4, :].bitcast(F32), ALU.subtract).then_inc(nlo, 1)

            dve.wait_ge(rel_in, 32)
            dve.wait_ge(const, 1)
            dve.tensor_copy(relb[:, :, :], relx[:, :].unsqueeze(2).broadcast_to([BUCKETS + 1, HEADS, P]))\
               .then_inc(relb_ready, 1)
            dve.wait_ge(prm_in, 16)
            dve.wait_ge(x_in, 16)
            freed(dve, ("ssq1",))
            normalise(C_N1, 0)
            for g in range(LEAD):
                lo_of(g)

            def glu(b):
                job_done(dve, ("glu", 2 * b + 1))
                freed(dve, ("glu", 2 * b))
                dve.scalar_tensor_tensor(out=u_pad[:, b, TAPS - 1:], in0=bank[BANK_OF[("glu", 2 * b + 1)]][:, 0:T],
                                         scalar=prm[:, C_GLU + b:C_GLU + b + 1], in1=sig[:, b, :],
                                         op0=ALU.add, op1=ALU.mult).then_inc(dve_evac, 1)

            def conv_tap(w):
                for b in range(CB):
                    src = u_pad[:, b, w:w + T]
                    wt = prm[:, C_DW + b * TAPS + w:C_DW + b * TAPS + w + 1]
                    if w == 0:
                        dve.wait_ge(const, 5)
                        freed(dve, ("glu", 2 * b + 1))
                        dve.tensor_scalar(acc[:, b, :], src, wt, prm[:, C_DWB + b:C_DWB + b + 1], ALU.mult, ALU.add)\
                           .then_inc(tap, 1)
                    else:
                        dve.wait_ge(tap, CB * (w - 1) + b + 1)
                        dve.scalar_tensor_tensor(out=acc[:, b, :], in0=src, scalar=wt, in1=acc[:, b, :],
                                                 op0=ALU.mult, op1=ALU.add).then_inc(tap, 1)

            def qk_norm(gi):
                freed(dve, ("qkssq", gi))
                link(dve.reciprocal(rs[:, gi % 2, :], rs[:, gi % 2, :]))
                two = qk[:, 2 * gi:2 * gi + 2, :].rearrange("p a t -> p (a t)")
                gain = C_QG if gi < AB // 2 else C_KG
                dve.scalar_tensor_tensor(out=two, in0=two, scalar=prm[:, gain:gain + 1], in1=rs[:, gi % 2, :],
                                         op0=ALU.mult, op1=ALU.mult).then_inc(qk_normed, 1)

            def score(s):
                c, pair = divmod(s, len(PAIRS))
                h0 = PAIRS[pair][0]
                w = P * (c + 1)
                pr = p3[:, h0:h0 + 3:2, c * P:c * P + w]
                ps = bank[BANK_OF[("score", s)]][:, 0:2 * w].rearrange("p (a n) -> p a n", a=2)
                job_done(dve, ("score", s))
                dve.scalar_tensor_tensor(out=pr, in0=ps, scalar=HD ** -0.5, in1=bias[:, h0:h0 + 3:2, T - w:T],
                                         op0=ALU.mult, op1=ALU.add).then_inc(dve_evac, 1)
                freed(dve, ("score", s))
                dve.tensor_reduce(negm[:, c * HEADS + h0:c * HEADS + h0 + 3:2], pr, AX.X, ALU.max, negate=True)\
                   .then_inc(score_max, 1)

            for n in range(T_CONV):
                lo_of(n + LEAD)
                if n < T_QK:
                    if n % 2:
                        glu(n // 2)
                elif n < T_QK + TAPS:
                    conv_tap(n - T_QK)
                if n >= T_QK + 4 and n % 2 == 0 and (n - T_QK - 4) // 2 < AB:
                    qk_norm((n - T_QK - 4) // 2)
                if n == 34:
                    dve.wait_ge(bias_in, 16 * HEADS)
                if 34 <= n < 40:
                    score(2 * (n - 34))
                    score(2 * (n - 34) + 1)
            job_done(dve, ("lnsum",))
            dve.wait_ge(tap, CB * TAPS)
            dve.tensor_scalar(rs[:, 1, 0:T], bank[BANK_OF[("lnsum",)]][:, 0:T], 1.0 / CONV_CH, None, ALU.mult)\
               .then_inc(dve_evac, 1)
            freed(dve, ("lnsum",))
            dve.tensor_tensor(u_pad[:, :, 0:T], acc[:, :, :], rs[:, 1:2, 0:T].broadcast_to([P, CB, T]), ALU.subtract)\
               .then_inc(centred, 1)
            dve.wait_ge(lns, 1)
            link(dve.tensor_tensor(lse[:, :], lnl[:, :], negm[:, :], ALU.subtract))
            lse4 = lse[:, :].rearrange("p (c g s) -> p c s g", c=TC, g=GROUPS)
            for c in range(TC):
                link(dve.tensor_reduce(gmax[:, c * SLOTS:(c + 1) * SLOTS], lse4[:, c], AX.X, ALU.max))
            for c in range(TC):
                l3 = lse[:, c * HEADS:(c + 1) * HEADS].rearrange("p (g s) -> p g s", g=GROUPS)
                m3 = gmax[:, c * SLOTS:(c + 1) * SLOTS].unsqueeze(1).broadcast_to([P, GROUPS, SLOTS])
                dve.tensor_tensor(l3, l3, m3, ALU.subtract).then_inc(wexp, 1)
            dve.wait_ge(lns, 2)
            ew4 = ew[:, :].rearrange("p (c g s) -> p c s g", c=TC, g=GROUPS)
            for c in range(TC):
                link(dve.tensor_reduce(gsum[:, c * SLOTS:(c + 1) * SLOTS], ew4[:, c], AX.X, ALU.add))
            for c in range(TC):
                z3 = zz[:, c * HEADS:(c + 1) * HEADS].rearrange("p (g s) -> p g s", g=GROUPS)
                l3 = lsum[:, c * HEADS:(c + 1) * HEADS].rearrange("p (g s) -> p g s", g=GROUPS)
                g3 = gsum[:, c * SLOTS:(c + 1) * SLOTS].unsqueeze(1).broadcast_to([P, GROUPS, SLOTS])
                link(dve.tensor_tensor(z3, l3, g3, ALU.mult))
            link(dve.reciprocal(fac[:, :], zz[:, :]))
            link(dve.tensor_tensor(fac[:, :], fac[:, :], ew[:, :], ALU.mult))
            for h in range(HEADS):
                for c in range(TC):
                    pr = p3[:, h, c * P:(c + 1) * P + c * P]
                    col = c * HEADS + h
                    dve.tensor_scalar(pr, pr, fac[:, col:col + 1], None, ALU.mult).then_inc(scaled, 1)
            freed(dve, ("lnvar",))
            link(dve.reciprocal(rs[:, 0, 0:T], rs[:, 0, 0:T]))
            dve.tensor_tensor(acc[:, :, :], u_pad[:, :, 0:T], rs[:, 0:1, 0:T].broadcast_to([P, CB, T]), ALU.mult)\
               .then_inc(ln_out, 1)
            dve.wait_ge(cu_h, 1)
            dve.tensor_tensor(cu_lo[:, :, :], acc[:, :, :], cu_hi[:, :, :].bitcast(F32), ALU.subtract).then_inc(cu_l, 1)
            for b in range(AB):
                dve.wait_ge(o_hi_ready, b + 1)
                dve.tensor_tensor(o_lo[:, b, :], bank[BANK_OF[("o", b)]][:, 0:T], o_hi[:, b, :].bitcast(F32),
                                  ALU.subtract).then_inc(dve_evac, 1)
            for b in range(KB):
                if b % 2 == 0:
                    lo_of(T_CONV + b // 2 + LEAD)
                job_done(dve, ("conv", b))
                dve.wait_ge(gates_ready, 1)
                dve.scalar_tensor_tensor(out=gsig[:, b, :], in0=bank[BANK_OF[("conv", b)]][:, 0:T],
                                         scalar=prm[:, C_BP + b:C_BP + b + 1], in1=gsig[:, b, :],
                                         op0=ALU.add, op1=ALU.mult).then_inc(dve_evac, 1)
            dve.wait_ge(gates_ready, 2)
            for b in range(KB):
                if T_ATT + b < T_MIX:
                    lo_of(T_ATT + b + LEAD)
                job_done(dve, ("attn", b))
                dve.tensor_tensor(gsig[:, KB + b, :], bank[BANK_OF[("attn", b)]][:, 0:T], gsig[:, KB + b, :],
                                  ALU.mult).then_inc(dve_evac, 1)
                freed(dve, ("attn", b))
                dve.tensor_tensor(gsig[:, b, :], gsig[:, b, :], gsig[:, KB + b, :], ALU.add).then_inc(merged, 1)
                dve.wait_ge(m_hi, b + 1)
                dve.wait_ge(merged, b + 1)
                dve.tensor_tensor(nrm_lo[:, b, :], gsig[:, b, :], nrm_hi[:, b, :].bitcast(F32), ALU.subtract)\
                   .then_inc(m_lo, 1)
            for b in range(KB):
                lo_of(T_MIX + b + LEAD)
                job_done(dve, ("mix", b))
                dve.tensor_tensor(resid[:, b, :], bank[BANK_OF[("mix", b)]][:, 0:T], resid[:, b, :], ALU.add)\
                   .then_inc(dve_evac, 1)
            freed(dve, ("ssq2",))
            dve.wait_ge(dve_evac, FREED[("mix", KB - 1)])
            normalise(C_N2, 1)
            for u in range(HALVES):
                lo_of(T_WQ + u + LEAD)

            dve.wait_ge(const, 9)

            def top16(vals, idx, row):
                link(dve.max(vals[:, 0:8], row))
                link(dve.max_index(idx[:, 0:8], vals[:, 0:8], row))
                link(dve.match_replace(row, vals[:, 0:8], row, LOWEST))
                link(dve.max(vals[:, 8:16], row))
                link(dve.max_index(idx[:, 8:16], vals[:, 8:16], row))

            def candidates(c):
                t3 = topv[:, c * HALVES:(c + 1) * HALVES, :]
                link(dve.tensor_tensor(cand[:, :, :].rearrange("p h (a b) -> p h a b", a=TOPK),
                                       t3[:, 0::2, :].unsqueeze(3).broadcast_to([P, PH, TOPK, TOPK]),
                                       t3[:, 1::2, :].unsqueeze(2).broadcast_to([P, PH, TOPK, TOPK]), ALU.add))

            def lookup(c, w):
                pos = (cf1, cf2)[w][:, c * P:(c + 1) * P]
                e4 = eq[:, :].rearrange("p (h k j) -> p h k j", h=PH, k=TOPK)
                e3 = eq[:, :].rearrange("p (n j) -> p n j", j=TOPK)
                link(dve.tensor_tensor(e3, pos.unsqueeze(2).broadcast_to([P, PH * TOPK, TOPK]),
                                       iota[:, 0:TOPK].unsqueeze(1).broadcast_to([P, PH * TOPK, TOPK]), ALU.is_equal))
                tf = topf[:, c * HALVES + w:(c + 1) * HALVES:2, :].unsqueeze(2).broadcast_to([P, PH, TOPK, TOPK])
                link(dve.tensor_tensor(e4, e4, tf, ALU.mult))
                link(dve.tensor_reduce(sel[:, w, c, :], e3, AX.X, ALU.add))

            def top_step(i):
                if i < 2 * HALVES:
                    if i % 4 == 0:
                        freed(dve, ("sc", i // 4))
                    top16(topv[:, i, :], topi[:, i, :], S[:, i, :])
                elif i == 2 * HALVES:
                    link(dve.tensor_copy(topf[:, :, :], topi[:, :, :]))
                elif i < 2 * HALVES + 1 + 2 * 13:
                    c, r = divmod(i - 2 * HALVES - 1, 13)
                    both = slice(c * P, (c + 1) * P)
                    if r == 0:
                        candidates(c)
                    elif r <= PH:
                        u = c * PH + r - 1
                        top16(bestv[:, u, :], besti[:, u * TOPK:(u + 1) * TOPK], cand[:, r - 1, :])
                    elif r == PH + 1:
                        link(dve.tensor_scalar(bc1[:, both], besti[:, both], 4, None, ALU.logical_shift_right))
                        link(dve.tensor_scalar(bc2[:, both], besti[:, both], 15, None, ALU.bitwise_and))
                        link(dve.tensor_copy(cf1[:, both], bc1[:, both]))
                        link(dve.tensor_copy(cf2[:, both], bc2[:, both]))
                    elif r <= PH + 3:
                        lookup(c, r - PH - 2)
                    else:
                        b3 = bestv[:, c * PH:(c + 1) * PH, :]
                        x3 = ex[:, both].rearrange("p (u k) -> p u k", k=TOPK)
                        ins = dve.tensor_tensor(x3, b3, b3[:, :, 0:1].broadcast_to([P, PH, TOPK]), ALU.subtract)
                        if c:
                            ins.then_inc(top_done, 1)
                        else:
                            link(ins)

            for i in range(HALF - RING):
                if by_dve(U0 + LEAD, i):
                    split_lo(dve, U0 + LEAD, 0, i)
                top_step(i)
            for j in range(RING):
                if by_dve(U0 + HALF - RING + LEAD, j):
                    split_lo(dve, U0 + HALF - RING + LEAD, 0, j)
                if j == 0:
                    dve.wait_ge(gexp, 1)
                    e3 = ex[:, :].rearrange("p (u k) -> p u k", k=TOPK)
                    link(dve.tensor_reduce(zs[:, 0, :], e3, AX.X, ALU.add))
                    link(dve.reciprocal(zs[:, 1, :], zs[:, 0, :]))
                    dve.tensor_tensor(gate[:, :, :].rearrange("p c (u k) -> p (c u) k", k=TOPK), e3,
                                      zs[:, 1, :].unsqueeze(2).broadcast_to([P, TC * PH, TOPK]), ALU.mult)\
                       .then_inc(gate_ready, 1)
            dve.wait_ge(pick_T, 1)
            dve.tensor_copy(keys[:, :, :], bank[6][:, :].rearrange("p (a t) -> p a t", a=2)).then_inc(pick_ready, 1)
            dve.wait_ge(pick_T, 2)
            link(dve.tensor_copy(pickf[:, 0, :], bank[7][:, 0:T]))
            link(dve.tensor_copy(parts[:, 0, :], pickf[:, 0, :]))
            link(dve.tensor_tensor(pickf[:, 1, :], pickf[:, 0, :], parts[:, 0, :], ALU.subtract))
            link(dve.tensor_copy(parts[:, 1, :], pickf[:, 1, :]))
            dve.tensor_tensor(parts[:, 2, :], pickf[:, 1, :], parts[:, 1, :], ALU.subtract).then_inc(pick_ready, 1)
            dve.wait_ge(pick_ready, 2)
            dve.wait_ge(const, 10)

            def one_hots(half, it, j):
                n = it * 4 + (half * HALF + j)
                t = bass.ds(it * (4 * TOK) + j * TOK, TOK)
                wait(dve, gate_mm, n - 1)

                def at(x, m):
                    return x.unsqueeze(1).broadcast_to([P, m, TOK])

                dve.tensor_tensor(eqB[:, j % 2], iota4[:, half * HALF:(half + 1) * HALF, :], at(keys[:, 1, t], HALF),
                                  ALU.is_equal).then_inc(second, 1)
                dve.tensor_tensor(ohA[:, j % 2], iota4[:, :, :], at(keys[:, 0, t], NK), ALU.is_equal)\
                   .then_inc(spread, 1)
                dve.wait_ge(second, n + 1)
                dve.tensor_tensor(ohB[:, j % 2], eqB[:, j % 2].unsqueeze(1).broadcast_to([P, 3, HALF, TOK]),
                                  parts[:, :, t].unsqueeze(2).broadcast_to([P, 3, HALF, TOK]), ALU.mult)\
                   .then_inc(spread, 1)

            def multiply(half, it, j):
                n = it * 4 + (half * HALF + j)
                wait(dve, gate_mm, n + 1)
                av = act[:, half * HALF:(half + 1) * HALF, bass.ds(it * (4 * TOK) + j * TOK, TOK)]
                gv = bank[6 + j % 2][:, 0:TOK * HALF].rearrange("p (q n) -> p n q", q=TOK)
                dve.tensor_tensor(av, av, gv, ALU.mult).then_inc(gated, 1)

            def low_part(base_i, it, j):
                dve.wait_ge(a_hi, it * 4 + (base_i + j + 1))
                s = (base_i + j) % RING
                dve.tensor_tensor(nrm_lo[:, s, :], act[:, it * 4 + (base_i + j), :], nrm_hi[:, s, :].bitcast(F32),
                                  ALU.subtract).then_inc(a_lo, 1)

            def gate_body(half, it, first=False, last=False):
                base = U0 + HALF if half == 0 else V0
                for j in range(RING):
                    if half == 1 and not (last and j == RING - 1):
                        low_part(1, it, j)
                    if by_dve(base + LEAD, j):
                        split_lo(dve, base + LEAD, it, j)
                    one_hots(half, it, j)
                    if j:
                        multiply(half, it, j - 1)
                    elif not first:
                        multiply(half, it - 1, RING - 1)

            for half in range(2):
                dve.wait_ge(gelu_done, HALF * (half + 1))
                if half == 1:
                    low_part(0, 0, 0)
                gate_body(half, 0, first=True)
                with dve.Fori(1, HALF // RING - 1) as it:
                    gate_body(half, it)
                gate_body(half, HALF // RING - 1, last=True)
                multiply(half, HALF // RING - 1, RING - 1)
            low_part(HALF, 0, 0)
            with dve.Fori(0, HALF // RING - 1) as it:
                for j in range(RING):
                    low_part(HALF + 1, it, j)
                    if by_dve(V0 + HALF + LEAD, j):
                        split_lo(dve, V0 + HALF + LEAD, it, j)
            for j in range(RING - 1):
                low_part(N_V - RING + 1, 0, j)
                if j == 0:
                    split_lo(dve, V0 + N_V - 1, 0, 0)
            dve.wait_ge(pe_step, S_V + N_V)
            for half in range(2):
                dve.tensor_copy(yout[:, 512 * half:512 * half + 512], bank[half][:, :]).then_inc(y_dve, 1)

        @block.tensor
        def _(pe):
            done = [0]

            def step(ins):
                done[0] += 1
                ins.then_inc(pe_step, 1)

            def start(job):
                i = JOBS.index(job)
                if i >= 8:
                    freed(pe, JOBS[i - 8])
                return bank[BANK_OF[job]]

            def product(dst, s, units, vec_hi, vec_lo, base, it, j, first=True, last=True):
                wait_lo(pe, base, it, j)
                n = len(units)
                for i, (u, k) in enumerate(units):
                    for p_, (w_, x_) in enumerate(((hi, vec_hi), (hi, vec_lo), (lo, vec_hi))):
                        ins = pe.matmul(dst, w_[:, s, u * P:(u + 1) * P], x_[:, k, :],
                                        start=first and i == 0 and p_ == 0, stop=last and i == n - 1 and p_ == 2)
                return ins

            def full(n, job):
                b = start(job)
                return product(b[:, 0:T], n % RING, [(k, k) for k in range(KB)], nrm_hi, nrm_lo, n, 0, 0)

            pe.wait_ge(const, 7)
            b = start(("ssq1",))
            for k in range(KB):
                pe.wait_ge(squared, k // 4 + 1)
                ins = pe.matmul(b[:, 0:T], ones[:, :], sq[:, k, :], start=k == 0, stop=k == KB - 1)
            step(ins)
            pe.wait_ge(relb_ready, 1)
            pe.wait_ge(rel_in, 32)
            for h in range(HEADS):
                b = start(("bias", h))
                step(pe.matmul(b[:, 0:BW], relb[:, h, :], oneh[:, h // SLOTS, :], start=True, stop=True))
            pe.wait_ge(nlo, 2)

            def qk_sums(gi):
                b = start(("qkssq", gi))
                pe.wait_ge(qk_sq, 2 * gi + 2)
                for r in range(2):
                    ins = pe.matmul(b[:, r * T:(r + 1) * T], bones[:, :], sq[:, (2 * gi + r) % KB, :],
                                    start=r == 0, stop=True, skip_group_check=True)
                step(ins)

            def turn_v(i):
                b = start(("vt", i))
                pe.wait_ge(const, 8)
                for r in range(2):
                    freed(pe, ("v", 2 * i + r))
                    for c in range(TC):
                        ins = pe.transpose(b[:, (2 * r + c) * P:(2 * r + c + 1) * P],
                                           vT[:, (2 * i + r) % CB, c * P:(c + 1) * P], ident[:, :])
                step(ins)

            def scores(s):
                c, pair = divmod(s, len(PAIRS))
                w = P * (c + 1)
                b = start(("score", s))
                pe.wait_ge(qk_normed, AB)
                for r, h in enumerate(PAIRS[pair]):
                    rows = slice((h % 2) * HD, (h % 2 + 1) * HD)
                    ins = pe.matmul(b[:, r * w:(r + 1) * w], qk[rows, h // 2, c * P:(c + 1) * P],
                                    qk[rows, AB + h // 2, 0:w], start=r == 0, stop=True, skip_group_check=True)
                step(ins)

            for n in range(T_CONV):
                if n < T_QK:
                    step(full(n, ("glu", n)))
                elif n < T_V:
                    step(full(n, ("qk", n - T_QK)))
                elif n < T_GATE:
                    step(full(n, ("v", n - T_V)))
                else:
                    step(full(n, ("gate", n - T_GATE)))
                if n >= T_QK + 3 and (n - T_QK - 3) % 2 == 0 and (n - T_QK - 3) // 2 < AB:
                    qk_sums((n - T_QK - 3) // 2)
                if n >= T_V + 2 and n % 2 == 0 and n <= T_V + AB:
                    turn_v((n - T_V - 2) // 2)
                if 33 <= n < 39:
                    scores(2 * (n - 33))
                    scores(2 * (n - 33) + 1)
                if n == 39:
                    b = start(("lnsum",))
                    pe.wait_ge(tap, CB * TAPS)
                    for k in range(CB):
                        ins = pe.matmul(b[:, 0:T], ones[:, :], acc[:, k, :], start=k == 0, stop=k == CB - 1)
                    step(ins)
                if n == 41:
                    b = start(("lnvar",))
                    pe.wait_ge(centred_sq, 1)
                    for k in range(CB):
                        ins = pe.matmul(b[:, 0:T], ones[:, :], sq[:, k, :], start=k == 0, stop=k == CB - 1)
                    step(ins)

            def turn(h):
                b = start(("pT", h))
                pe.wait_ge(scaled, 2 * h + 2)
                pe.wait_ge(const, 8)
                for r in range(3):
                    ins = pe.transpose(b[:, r * P:(r + 1) * P], p3[:, h, r * P:(r + 1) * P], ident[:, :])
                step(ins)

            freed(pe, ("vt", AB // 2 - 1))

            def attend(bl):
                b = start(("o", bl))
                for r in range(2):
                    h = 2 * bl + r
                    freed(pe, ("pT", h))
                    dst = b[r * HD:(r + 1) * HD, 0:T]
                    vv = [v[:, c, h * HD:(h + 1) * HD] for c in range(TC)]
                    pe.matmul(dst[:, 0:P], vv[0], pT[:, h % 4, 0, :], start=True, stop=True, skip_group_check=True)
                    pe.matmul(dst[:, P:T], vv[0], pT[:, h % 4, 1, :], start=True, stop=False, skip_group_check=True)
                    ins = pe.matmul(dst[:, P:T], vv[1], pT[:, h % 4, 2, :], start=False, stop=True,
                                    skip_group_check=True)
                step(ins)

            for bl in range(AB):
                turn(2 * bl)
                turn(2 * bl + 1)
                if bl:
                    attend(bl - 1)
            attend(AB - 1)
            pe.wait_ge(cu_l, 1)
            for b_ in range(KB):
                n = T_CONV + b_ // 2
                b = start(("conv", b_))
                step(product(b[:, 0:T], n % RING, [((b_ % 2) * CB + k, k) for k in range(CB)], cu_hi, cu_lo, n, 0, 0))
            freed(pe, ("o", AB - 1))
            for b_ in range(KB):
                b = start(("attn", b_))
                units = list(range(AB * b_, AB * b_ + AB))
                for tile in sorted({u // 8 for u in units}):
                    mine = [u for u in units if u // 8 == tile]
                    n = T_ATT + tile
                    ins = product(b[:, 0:T], n % RING, [(u % 8, u % AB) for u in mine], o_hi, o_lo, n, 0, 0,
                                  first=mine[0] == units[0], last=mine[-1] == units[-1])
                    if mine[-1] == units[-1] or mine[-1] % 8 == 7:
                        step(ins)
            pe.wait_ge(m_lo, KB)
            for b_ in range(KB):
                step(full(T_MIX + b_, ("mix", b_)))
            b = start(("ssq2",))
            for k in range(KB):
                pe.wait_ge(squared, 2 + k + 1)
                ins = pe.matmul(b[:, 0:T], ones[:, :], sq[:, k, :], start=k == 0, stop=k == KB - 1)
            step(ins)
            pe.wait_ge(nlo, 4)
            for u in range(HALVES):
                step(full(T_WQ + u, ("wq", u)))
            assert done[0] == FRONT_STEPS
            pe.wait_ge(sk_in, 16)
            for j in range(N_SC):
                b = start(("sc", j))
                for r in range(4):
                    c, u = divmod(4 * j + r, HALVES)
                    freed(pe, ("wq", u))
                    ins = pe.matmul(b[:, r * NK:(r + 1) * NK], qT[:, u, c * P:(c + 1) * P], skT[:, u, :],
                                    start=r == 0, stop=True, skip_group_check=True)
                ins.then_inc(sc_ready, 1)
            for j in range(N_SC):
                freed(pe, ("sc", j))

            for c in range(TC):
                for k in range(KB):
                    ins = pe.matmul(bank[2 * c + k // 4][:, (k % 4) * P:(k % 4 + 1) * P], resid[:, k, c * P:(c + 1) * P],
                              ident[:, :], start=k % 4 == 0, stop=False, skip_group_check=True)
            ins.then_inc(y_began, 1)

            def u_tile(base_i, it, j):
                wait(pe, gelu_done, it * 4 + (base_i + j - 1))
                ins = product(bank[4 + j % 2][:, 0:T], j, [(k, k) for k in range(KB)], nrm_hi, nrm_lo, U0 + base_i, it, j)
                ins.then_inc(pe_step, 1)

            def gates(half, it, j):
                n = it * 4 + (half * HALF + j)
                wait(pe, gated, n - 1)
                pe.wait_ge(spread, n * 2 + 2)
                for q in range(TOK):
                    for i in range(3):
                        ins = pe.matmul(bank[6 + j % 2][:, q * HALF:(q + 1) * HALF], ohA[:, j % 2, :, q],
                                        ohB[:, j % 2, i, :, q], start=i == 0, stop=i == 2, skip_group_check=True)
                ins.then_inc(gate_mm, 1)

            for j in range(RING):
                u_tile(0, 0, j)
            with pe.Fori(1, HALF // RING) as it:
                for j in range(RING):
                    u_tile(0, it, j)
            pe.wait_ge(top_done, 1)
            for w in range(2):
                for c in range(TC):
                    ins = pe.transpose(bank[6][:, w * T + c * P:w * T + (c + 1) * P], sel[:, w, c, :], ident[:, :])
            ins.then_inc(pick_T, 1)
            pe.wait_ge(gate_ready, 1)
            for c in range(TC):
                ins = pe.transpose(bank[7][:, c * P:(c + 1) * P], gate[:, c, :], ident[:, :])
            ins.then_inc(pick_T, 1)

            def u_and_gates(it):
                for j in range(RING):
                    u_tile(HALF, it, j)
                    gates(0, it, j)

            u_and_gates(0)
            with pe.Fori(1, HALF // RING) as it:
                u_and_gates(it)

            def v_tile(base_i, it, j, stop=False):
                wait_lo(pe, V0 + base_i, it, j)
                pe.wait_ge(a_lo, it * 4 + (base_i + j + 1))
                for c in range(TC):
                    for a_, v_ in ((nrm_hi, hi), (nrm_hi, lo), (nrm_lo, hi)):
                        for half in range(2):
                            ins = pe.matmul(bank[2 * c + half][:, :], a_[:, j, c * P:(c + 1) * P],
                                            v_[:, j, half * 512:(half + 1) * 512],
                                            start=False, stop=stop and a_ is nrm_lo, skip_group_check=True)
                ins.then_inc(pe_step, 1)

            def v_and_gates(it):
                for j in range(RING):
                    v_tile(0, it, j)
                    gates(1, it, j)

            v_and_gates(0)
            with pe.Fori(1, HALF // RING) as it:
                v_and_gates(it)
            with pe.Fori(0, HALF // RING - 1) as it:
                for j in range(RING):
                    v_tile(HALF, it, j)
            for j in range(RING):
                v_tile(N_V - RING, 0, j, stop=j == RING - 1)


def bucket_rows():
    n = 255 - np.arange(BW)
    exact = BUCKETS // 2
    nf = np.maximum(n, 1).astype(np.float32)
    large = exact + (np.log(nf / np.float32(exact)) / np.float32(np.log(MAX_DISTANCE / exact))
                     * np.float32(BUCKETS - exact)).astype(np.int32)
    bucket = np.where(n < exact, n, np.minimum(large, BUCKETS - 1))
    rows = np.zeros((BUCKETS + 1, GROUPS, BW), np.float32)
    for g, (window, dilation) in enumerate(WINDOWS):
        valid = (n >= 0) & (n <= window) & (n % dilation == 0)
        rows[np.where(valid, bucket, BUCKETS), g, np.arange(BW)] = 1.0
    return rows


def kernel(**inputs):
    from concourse.bacc import Bacc
    from concourse.bass_utils import run_bass_kernel_spmd

    a = {k: np.asarray(x) for k, x in inputs.items()}

    def tiles(w, blocks):
        k = w.shape[0] // P
        return w.reshape(k, P, -1, P).transpose(2, 0, 1, 3)[blocks].reshape(-1, 8, P, P)\
                .transpose(0, 2, 1, 3).reshape(-1, P, 8 * P)

    glu = [b for pair in zip(range(CB, 2 * CB), range(CB)) for b in pair]
    n_in = a["w_in"].shape[2] // P
    front = np.concatenate([
        tiles(a["w_in"][0], glu + list(range(2 * CB, n_in))),
        tiles(a["conv_w_proj"][0], list(range(KB))),
        tiles(a["attn_w_proj"][0], list(range(KB))),
        tiles(a["mix_w_out"][0], list(range(KB))),
        tiles(a["peer_w_q"][0], list(range(HALVES))),
    ])

    def col(x):
        return x.reshape(-1, P).T

    cols = np.concatenate([
        col(a["norm1_g"][0]), col(a["norm2_g"][0]), col(a["conv_b_glu"][0]),
        a["conv_dw_w"][0, :, 0].reshape(TAPS, CB, P).transpose(2, 1, 0).reshape(P, CB * TAPS),
        col(a["conv_dw_b"][0]), col(a["conv_ln_g"][0]), col(a["conv_ln_b"][0]), col(a["conv_b_proj"][0]),
        np.tile(a["q_norm_g"][0], 2)[:, None], np.tile(a["k_norm_g"][0], 2)[:, None],
    ], axis=1)
    arrays = {
        "x_t": a["x"][0].T.reshape(KB, P, T).transpose(1, 0, 2),
        "front": front,
        "cols": cols,
        "rel_bias": a["rel_bias"],
        "onehot": bucket_rows(),
        "sub_keys": a["peer_sub_keys"][0].reshape(HALVES, NK, P).transpose(2, 0, 1),
        "u_tiles": a["peer_u"][0].reshape(NK, NK, KB, P).transpose(1, 3, 2, 0).reshape(NK, P, D),
        "v_tiles": a["peer_v"][0].reshape(NK, NK, D).transpose(1, 0, 2),
    }
    arrays = {k: np.ascontiguousarray(x) for k, x in arrays.items()}
    nc = Bacc("TRN2", target_bir_lowering=False, num_devices=1)
    args = [nc.dram_tensor(k, x.shape, mybir.dt.from_np(x.dtype), kind="ExternalInput").ap()
            for k, x in arrays.items()]
    y = nc.dram_tensor("y", (TC, P, D), F32, kind="ExternalOutput").ap()
    hybrid_block(nc, *args, y)
    r = run_bass_kernel_spmd(nc, [arrays], core_ids=[0])
    return r.results[0]["y"].reshape(1, T, D)
```

```python
from contextlib import ExitStack

import numpy as np

import concourse.bass as bass
from concourse import mybir

F32 = mybir.dt.float32
F32R = mybir.dt.float32r
U32 = mybir.dt.uint32
BF16 = mybir.dt.bfloat16
ALU = mybir.AluOpType
ACT = mybir.ActivationFunctionType
AX = mybir.AxisListType

P = 128
D = 1024
T = 256
KB = D // P
TC = T // P
CONV_CH, TAPS = 512, 31
CB = CONV_CH // P
HEADS, HD = 12, 64
SLOTS, GROUPS = 4, 3
AW = HEADS * HD
AB = AW // P
WINDOWS = ((128, 1), (512, 4), (2048, 16))
BUCKETS, MAX_DISTANCE = 32, 2048
PH, NK, TOPK = 8, 128, 16
HALVES = 2 * PH
EPS = 1e-6
NEG = -1e30
LOWEST = -3.0e38
BW = 384

T_GLU, T_QK, T_V, T_GATE = 0, 8, 20, 26
T_CONV, T_ATT, T_MIX, T_WQ = 42, 46, 52, 60
N_FRONT = 76
N_U = N_V = NK
RING = 4
LEAD = 3
CHUNK_STEPS = PH // 2 + 9
TOP_TILES = 48
EXP_TILE = 52
PICK_TILE = 60
HALF = NK // 2
TOK = 4


BIAS_AT = {1: (7, 8, 9), 2: (10, 11)}
QSS_AT, KSS_AT, KB_AT = 15, 20, 22
VT_AT = {22: 0, 24: 1, 26: 2}
SCORES_AT = {24: (0, 1), 25: (2, 3), 26: (4, 5), 27: (6,), 28: (7,), 29: (8,), 30: (9,), 31: (10,), 32: (11,)}
LNSUM_AT, LNVAR_AT = 37, 40
WEIGHTS_AT = 35
TAPS_AT = {}
for _w in range(TAPS):
    TAPS_AT.setdefault(T_QK + (_w * 4 // 5 if _w < 18 else 14 + _w - 17), []).append(_w)


def jobs_in_order():
    order = [(("bias", 0), None), (("bias", 1), None), (("ssq1",), None)]
    order += [(("bias", h), None) for h in range(2, 7)]
    for n in range(T_CONV):
        if n < T_QK:
            order.append((("glu", n), n))
        elif n < T_V:
            order.append((("qk", n - T_QK), n))
        elif n < T_GATE:
            order.append((("v", n - T_V), n))
        else:
            order.append((("gate", n - T_GATE), n))
        order += [(("bias", h), None) for h in BIAS_AT.get(n, ())]
        if n == QSS_AT:
            order.append((("qss",), None))
        if n == KSS_AT:
            order.append((("kss",), None))
        if n == KB_AT:
            order += [(("kb", i), None) for i in range(AB // 2)]
        if n in VT_AT:
            order.append((("vt", VT_AT[n]), None))
        order += [(("score", i), None) for i in SCORES_AT.get(n, ())]
        if n == LNSUM_AT:
            order.append((("lnsum",), None))
        if n == LNVAR_AT:
            order.append((("lnvar",), None))
    for b in range(AB):
        order += [(("pT", 2 * b), None), (("pT", 2 * b + 1), None)]
        if b:
            order.append((("o", b - 1), None))
    order.append((("o", AB - 1), None))
    for n in range(CB):
        order += [(("conv", 2 * n), None), (("conv", 2 * n + 1), T_CONV + n)]
    for b in range(KB):
        for u in range(AB * b, AB * b + AB):
            if u % 8 == 7 and u != AB * b + AB - 1:
                order.append((None, T_ATT + u // 8))
        last = AB * b + AB - 1
        order.append((("attn", b), T_ATT + last // 8 if last % 8 == 7 else None))
    order += [(("mix", b), T_MIX + b) for b in range(KB)]
    order.append((("ssq2",), None))
    order += [(("wq", u), T_WQ + u) for u in range(HALVES)]
    return order


ORDER = jobs_in_order()
STEP_OF_JOB = {job: i + 1 for i, (job, _) in enumerate(ORDER) if job}
STEP_OF_TILE = {tile: i + 1 for i, (_, tile) in enumerate(ORDER) if tile is not None}
FRONT_STEPS = len(ORDER)
N_SC = 2 * HALVES // 4
JOBS = [job for job, _ in ORDER if job] + [("sc", j) for j in range(N_SC)]
BANK_OF = {job: i % 8 for i, job in enumerate(JOBS)}
BY_DVE = ("kb", "score", "lnsum", "o", "conv", "attn", "mix")


def freed_by_dve(job):
    return job[0] in BY_DVE or (job[0] == "glu" and job[1] % 2 == 1)


FREED = {}
_n = {True: 0, False: 0}
for _job in JOBS:
    _n[freed_by_dve(_job)] += 1
    FREED[_job] = _n[freed_by_dve(_job)]

PAIRS = [(0, 2), (1, 3), (4, 6), (5, 7), (8, 10), (9, 11)]

C_N1, C_N2, C_GLU, C_DW, C_DWB = 0, 8, 16, 24, 24 + CB * TAPS
C_LNG = C_DWB + CB
C_LNB = C_LNG + CB
C_BP = C_LNB + CB
C_QG = C_BP + KB
C_KG = C_QG + 1
N_COLS = C_KG + 1


def hybrid_block(nc, x_t, front, cols, rel_bias, onehot, sub_keys, u_tiles, v_tiles, out):
    toeplitz = nc.dram_tensor("toeplitz", (HEADS, P * BW), F32, kind="Internal").ap()
    with ExitStack() as ctx:
        def sb(name, shape, dt=F32, stack=ctx):
            return stack.enter_context(nc.sbuf_tensor(name, shape, dt))

        def sem(name):
            return ctx.enter_context(nc.semaphore(name))

        bank = [ctx.enter_context(nc.psum_tensor(f"bank{i}", [P, 512], F32)) for i in range(8)]

        raw = sb("raw", [P, RING, D])
        hi = sb("hi", [P, RING, D], F32R)
        lo = sb("lo", [P, RING, D], F32R)
        nrm_hi = sb("nrm_hi", [P, KB, T], F32R)
        nrm_lo = sb("nrm_lo", [P, KB, T], F32R)
        ident = sb("ident", [P, P])
        iota = sb("iota", [P, TOPK])
        inner = ExitStack()

        def tmp(name, shape, dt=F32):
            return sb(name, shape, dt, inner)

        ones = tmp("ones", [P, P])
        prm = tmp("prm", [P, N_COLS])
        relx = tmp("relx", [BUCKETS + 1, HEADS])
        relb = tmp("relb", [BUCKETS + 1, HEADS, P])
        kmask = tmp("kmask", [P, 2 * HEADS - 2])
        ksel = tmp("ksel", [HEADS, AB, P])
        gains = tmp("gains", [P, 1])
        oneh = tmp("oneh", [BUCKETS + 1, GROUPS, BW])
        sq = tmp("sq", [P, KB, T])
        rs = tmp("rs", [P, 2, 512])
        u_pad = tmp("u_pad", [P, CB, TAPS - 1 + T])
        sig = tmp("sig", [P, CB, T])
        acc = tmp("acc", [P, CB, T])
        cu_hi = tmp("cu_hi", [P, CB, T], F32R)
        cu_lo = tmp("cu_lo", [P, CB, T], F32R)
        qk = tmp("qk", [P, 2 * AB, T])
        v = tmp("v", [P, TC, AW])
        vT = sig
        gsig = tmp("gsig", [P, 2 * KB, T])
        bias = tmp("bias", [P, HEADS, T])
        prob = tmp("prob", [P, HEADS * BW])
        pT = tmp("pT", [P, 4, 3, P])
        o_hi = tmp("o_hi", [P, AB, T], F32R)
        o_lo = tmp("o_lo", [P, AB, T], F32R)
        stat = tmp("stat", [P, 16, TC * HEADS])
        resid = tmp("resid", [P, KB, T])
        inner.close()
        act = sb("act", [P, NK, T])
        iota4 = sb("iota4", [P, NK, TOK], BF16)
        keys = sb("keys", [P, 2, T], BF16)
        parts = sb("parts", [P, 3, T], BF16)
        ohA = sb("ohA", [P, 2, NK, TOK], BF16)
        eqB = sb("eqB", [P, 2, HALF, TOK], BF16)
        ohB = sb("ohB", [P, 2, 3, HALF, TOK], BF16)

        p3 = prob[:, :].rearrange("p (h n) -> p h n", n=BW)
        qT = prob[:, 0:HALVES * T].rearrange("p (u t) -> p u t", t=T)
        skT = qk[:, 0:HALVES // 2, :].rearrange("p a t -> p (a t)").rearrange("p (u n) -> p u n", n=NK)
        negm, lsum, lnl, lse, ew, zz, fac = [stat[:, i, :] for i in range(7)]
        rq = stat[:, 9, :]
        rk = rs[0:HEADS, 1, 0:T]
        gmax, gsum = stat[:, 7, 0:TC * SLOTS], stat[:, 8, 0:TC * SLOTS]
        def part(t0, n):
            return act[:, t0:t0 + n, :].rearrange("p a t -> p (a t)")

        S = part(112, 16).rearrange("p (u n) -> p u n", n=NK)
        cand = part(104, 8).rearrange("p (h n) -> p h n", n=TOPK * TOPK)
        eq = part(96, 8)
        topv = part(64, 2).rearrange("p (u k) -> p u k", k=TOPK)
        topi = part(66, 2).bitcast(U32).rearrange("p (u k) -> p u k", k=TOPK)
        topf = part(68, 2).rearrange("p (u k) -> p u k", k=TOPK)
        bestv = part(70, 1).rearrange("p (u k) -> p u k", k=TOPK)
        besti = part(71, 1).bitcast(U32)
        bc1 = part(72, 1).bitcast(U32)
        bc2 = part(73, 1).bitcast(U32)
        cf1 = part(74, 1)
        cf2 = part(75, 1)
        sel = part(76, 2).rearrange("p (w c n) -> p w c n", w=2, c=TC)
        ex = part(78, 1)
        gate = part(79, 1).rearrange("p (c n) -> p c n", c=TC)
        pickf = part(81, 4).rearrange("p (a t) -> p a t", a=4)
        zs = part(80, 1)[:, 0:3 * TC * PH].rearrange("p (a n) -> p a n", a=3)
        yout = part(0, 8)

        raw_in = [sem(f"raw_in{i}") for i in range(RING)]
        x_in = [sem(f"x_in{i}") for i in range(2)]
        prm_in, rel_in, bias_out, bias_in, sk_in, y_out = [sem(s) for s in (
            "prm_in", "rel_in", "bias_out", "bias_in", "sk_in", "y_out")]
        hi_ready, lo_pool, lo_dve = sem("hi_ready"), sem("lo_pool"), sem("lo_dve")
        pe_step = sem("pe_step")
        act_evac, dve_evac = sem("act_evac"), sem("dve_evac")
        const = sem("const")
        squared = sem("squared")
        normed = sem("normed")
        nhi, nlo = sem("nhi"), sem("nlo")
        relb_ready = sem("relb_ready")
        sig_ready = sem("sig_ready")
        qk_sq = sem("qk_sq")
        qk_normed = sem("qk_normed")
        gains_ready, rk_ready, rq_ready = sem("gains_ready"), sem("rk_ready"), sem("rq_ready")
        tap = sem("tap")
        score_max, exps, lns, wexp, scaled = sem("score_max"), sem("exps"), sem("lns"), sem("wexp"), sem("scaled")
        o_hi_ready = sem("o_hi_ready")
        centred, centred_sq, ln_out, silu, cu_h, cu_l, biased = [sem(s) for s in (
            "centred", "centred_sq", "ln_out", "silu", "cu_h", "cu_l", "biased")]
        gates_ready = sem("gates_ready")
        merged, m_hi, m_lo = sem("merged"), sem("m_hi"), sem("m_lo")
        chain = sem("chain")
        sc_ready = sem("sc_ready")
        gelu_done = sem("gelu_done")
        top_done, gexp, gate_ready, pick_T, pick_ready = [sem(s) for s in (
            "top_done", "gexp", "gate_ready", "pick_T", "pick_ready")]
        second, spread, gate_mm, gated = sem("second"), sem("spread"), sem("gate_mm"), sem("gated")
        a_hi, a_lo = sem("a_hi"), sem("a_lo")
        y_began, y_first = sem("y_began"), sem("y_first")
        y_dve, y_act = sem("y_dve"), sem("y_act")

        def wait(eng, s, value):
            if not isinstance(value, int) or value > 0:
                eng.wait_ge(s, value)

        def freed(eng, job):
            wait(eng, dve_evac if freed_by_dve(job) else act_evac, FREED[job])

        def job_done(eng, job):
            eng.wait_ge(pe_step, STEP_OF_JOB[job])

        def step_of(base, it, j):
            if isinstance(it, int) and base + 4 * it + j < N_FRONT:
                return STEP_OF_TILE[base + 4 * it + j]
            return it * 4 + (FRONT_STEPS + base + j - N_FRONT + 1)

        def slot_of(base, j):
            return (base + j) % RING

        def uses(base, it, j):
            return it + ((base + j) // RING + 1)

        def wait_raw(eng, base, it, j):
            eng.wait_ge(raw_in[slot_of(base, j)], uses(base, it, j) * 16)

        def split_hi(act_e, base, it, j):
            s = slot_of(base, j)
            wait_raw(act_e, base, it, j)
            if not (isinstance(it, int) and base + 4 * it + j < RING):
                wait(act_e, pe_step, step_of(base - 4, it, j))
            act_e.copy(hi[:, s, :], raw[:, s, :]).then_inc(hi_ready, 1)

        def by_dve(base, j):
            return slot_of(base, j) == 3

        def lo_count(base, it, j):
            if by_dve(base, j):
                return uses(base, it, j)
            return it * 3 + (3 * ((base + j) // RING) + slot_of(base, j) + 1)

        def wait_lo(eng, base, it, j):
            wait(eng, lo_dve if by_dve(base, j) else lo_pool, lo_count(base, it, j))

        def split_lo(eng, base, it, j):
            s = slot_of(base, j)
            eng.wait_ge(hi_ready, it * 4 + (base + j + 1))
            eng.tensor_tensor(lo[:, s, :], raw[:, s, :], hi[:, s, :].bitcast(F32), ALU.subtract)\
               .then_inc(lo_dve if by_dve(base, j) else lo_pool, 1)

        U0, V0 = N_FRONT, N_FRONT + N_U
        S_U, S_V = FRONT_STEPS, FRONT_STEPS + N_U

        block = ctx.enter_context(nc.Block())

        @block.sync
        def _(sp):
            sp.dma_start(oneh[:, :, :], onehot).then_inc(rel_in, 16)
            sp.dma_start(relx[0:BUCKETS, :], rel_bias).then_inc(rel_in, 16)
            for r in range(2):
                sp.dma_start(resid[:, 4 * r:4 * r + 4, :], x_t[:, 4 * r:4 * r + 4, :]).then_inc(x_in[r], 16)
            sp.dma_start(prm[:, :], cols).then_inc(prm_in, 16)

            def load(src, base, it, j):
                if not (isinstance(it, int) and base + 4 * it + j < RING):
                    wait_lo(sp, base - 4, it, j)
                sp.dma_start(raw[:, slot_of(base, j), :], src).then_inc(raw_in[slot_of(base, j)], 16)

            for g in range(N_FRONT):
                load(front[g], g, 0, 0)
                if 5 <= g < 5 + HEADS // 2:
                    for h in (2 * (g - 5), 2 * (g - 5) + 1):
                        freed(sp, ("bias", h))
                        sp.dma_start(toeplitz[h].rearrange("(p w) -> p w", w=BW), p3[:, h, :]).then_inc(bias_out, 16)
                if g == 14:
                    sp.wait_ge(bias_out, 16 * HEADS)
                if 14 <= g < 14 + HEADS // 2:
                    for h in (2 * (g - 14), 2 * (g - 14) + 1):
                        sp.dma_start(bias[:, h, :], toeplitz[h, P - 1:P - 1 + P * (BW - 1)].rearrange(
                            "(p w) -> p w", w=BW - 1)[:, 0:T]).then_inc(bias_in, 16)
                if g == T_MIX:
                    freed(sp, ("score", 11))
                    sp.dma_start(skT, sub_keys).then_inc(sk_in, 16)
            with sp.Fori(0, N_U // RING) as it:
                for j in range(RING):
                    load(u_tiles[it * RING + j], U0, it, j)
            with sp.Fori(0, N_V // RING) as it:
                for j in range(RING):
                    load(v_tiles[it * RING + j], V0, it, j)
            for c in range(TC):
                sp.wait_ge(y_dve, c + 1)
                sp.wait_ge(y_act, c + 1)
                sp.dma_start(out[c], yout[:, c * D:(c + 1) * D]).then_inc(y_out, 16)
            sp.wait_ge(y_out, 16 * TC)

        @block.gpsimd
        def _(pool):
            pool.memset(relx[BUCKETS:BUCKETS + 1, :], NEG).then_inc(const, 1)
            pool.wait_ge(const, 1)
            pool.memset(ones[:, :], 1.0).then_inc(const, 1)
            pool.memset(ident[:, :], 0.0).then_inc(const, 1)
            pool.memset(u_pad[:, :, 0:TAPS - 1], 0.0).then_inc(const, 1)
            pool.memset(kmask[:, :], 0.0).then_inc(const, 1)
            pool.wait_ge(const, 5)
            for r in range(2):
                pool.memset(kmask[r * HD:(r + 1) * HD, HEADS - 2 + r:HEADS - 1 + r], 1.0).then_inc(const, 1)
                pool.wait_ge(const, 6 + r)
            pool.affine_select(out=ident[:, :], in_=ident[:, :], compare_op=ALU.not_equal, fill=1.0,
                               base=0, pattern=[[-1, P]], channel_multiplier=1).then_inc(const, 1)
            pool.iota(iota[:, :], pattern=[[1, TOPK]], base=0, channel_multiplier=0,
                      allow_small_or_imprecise_dtypes=True).then_inc(const, 1)

            def lo_of(g):
                if not by_dve(g, 0):
                    split_lo(pool, g, 0, 0)

            for g in range(N_FRONT + LEAD):
                lo_of(g)
            pool.wait_ge(y_began, 1)
            pool.iota(iota4[:, :, :], pattern=[[1, NK], [0, TOK]], base=0, channel_multiplier=0,
                      allow_small_or_imprecise_dtypes=True).then_inc(const, 1)
            with pool.Fori(0, (N_U + N_V - RING) // RING) as it:
                for j in range(RING):
                    if not by_dve(U0 + LEAD, j):
                        split_lo(pool, U0 + LEAD, it, j)

        @block.scalar
        def _(a):
            def split_norm(k, round_):
                a.wait_ge(normed, KB * round_ + k + 1)
                a.copy(nrm_hi[:, k, :], sq[:, k, :]).then_inc(nhi, 1)

            def bias_rows(h):
                job_done(a, ("bias", h))
                a.copy(p3[:, h, :], bank[BANK_OF[("bias", h)]][:, 0:BW]).then_inc(act_evac, 1)

            a.preload_act_table(ACT.Sqrt)
            for r in range(2):
                a.wait_ge(x_in[r], 16)
                a.activation(sq[:, 4 * r:4 * r + 4, :], resid[:, 4 * r:4 * r + 4, :], ACT.Square)\
                 .then_inc(squared, 1)
            bias_rows(0)
            bias_rows(1)
            split_hi(a, 0, 0, 0)
            job_done(a, ("ssq1",))
            a.activation(rs[:, 0, 0:T], bank[BANK_OF[("ssq1",)]][:, 0:T], ACT.Sqrt, bias=EPS, scale=1.0 / D)\
             .then_inc(act_evac, 1)
            split_hi(a, 1, 0, 0)
            for k in range(KB):
                split_norm(k, 0)
                if k < 5:
                    bias_rows(2 + k)
            split_hi(a, 2, 0, 0)

            def exp_of(s):
                c, pair = divmod(s, len(PAIRS))
                w = P * (c + 1)
                a.wait_ge(score_max, s + 1)
                for h in PAIRS[pair]:
                    pr = p3[:, h, c * P:c * P + w]
                    col = c * HEADS + h
                    a.activation(pr, pr, ACT.Exp, bias=negm[:, col:col + 1],
                                 accum_out=lsum[:, col:col + 1]).then_inc(exps, 1)

            def evac_front(n):
                if n < T_QK:
                    if n % 2 == 0:
                        b = n // 2
                        job_done(a, ("glu", n))
                        a.activation(sig[:, b, :], bank[BANK_OF[("glu", n)]][:, 0:T], ACT.Sigmoid,
                                     bias=prm[:, C_GLU + CB + b:C_GLU + CB + b + 1]).then_inc(act_evac, 1)
                elif n < T_V:
                    i = n - T_QK
                    job_done(a, ("qk", i))
                    b = bank[BANK_OF[("qk", i)]][:, 0:T]
                    if i == KB:
                        job_done(a, ("qss",))
                    elif i == 0:
                        a.wait_ge(nhi, KB)
                        a.wait_ge(nlo, KB)
                    a.activation(sq[:, i % KB, :], b, ACT.Square).then_inc(qk_sq, 1)
                    a.copy(qk[:, i, :], b).then_inc(act_evac, 1)
                elif n >= T_GATE:
                    i = n - T_GATE
                    job_done(a, ("gate", i))
                    a.copy(gsig[:, i, :], bank[BANK_OF[("gate", i)]][:, 0:T]).then_inc(act_evac, 1)
                if T_V <= n < T_GATE:
                    i = n - T_V
                    job_done(a, ("v", i))
                    if i == 0:
                        freed(a, ("glu", 2 * CB - 1))
                    if i >= CB:
                        job_done(a, ("vt", (i - CB) // 2))
                    a.copy(vT[:, i % CB, :], bank[BANK_OF[("v", i)]][:, 0:T]).then_inc(act_evac, 1)
                for h in BIAS_AT.get(n, ()):
                    bias_rows(h)
                if n == QSS_AT:
                    job_done(a, ("qss",))
                    a.activation(rq[:, :], bank[BANK_OF[("qss",)]][:, 0:TC * HEADS], ACT.Sqrt, bias=HD * EPS)\
                     .then_inc(act_evac, 1)
                if n == KSS_AT:
                    job_done(a, ("kss",))
                    a.activation(rk, bank[BANK_OF[("kss",)]][0:HEADS, 0:T], ACT.Sqrt, bias=EPS, scale=1.0 / HD)\
                     .then_inc(act_evac, 1)
                if n in VT_AT:
                    i = VT_AT[n]
                    job_done(a, ("vt", i))
                    a.copy(v[:, :, 2 * i * P:(2 * i + 2) * P].rearrange("p c (b n) -> p b c n", b=2),
                           bank[BANK_OF[("vt", i)]][:, :].rearrange("p (b c n) -> p b c n", b=2, c=TC))\
                     .then_inc(act_evac, 1)

            for n in range(T_CONV):
                split_hi(a, n + LEAD, 0, 0)
                evac_front(n)
                for i in SCORES_AT.get(n - 2, ()):
                    exp_of(i)
                if n == WEIGHTS_AT:
                    a.wait_ge(exps, TC * HEADS)
                    a.activation(lnl[:, :], lsum[:, :], ACT.Ln).then_inc(lns, 1)
                if n == WEIGHTS_AT + 1:
                    a.wait_ge(wexp, TC)
                    a.activation(ew[:, :], lse[:, :], ACT.Exp).then_inc(lns, 1)
                if n == LNSUM_AT + 1:
                    job_done(a, ("kss",))
                    a.wait_ge(centred, 1)
                    a.activation(sq[:, 0:CB, :], u_pad[:, :, 0:T], ACT.Square).then_inc(centred_sq, 1)
                if n == LNVAR_AT:
                    job_done(a, ("lnvar",))
                    a.activation(rs[:, 0, 0:T], bank[BANK_OF[("lnvar",)]][:, 0:T], ACT.Sqrt, bias=EPS,
                                 scale=1.0 / CONV_CH).then_inc(act_evac, 1)

            def gate_sigmoid(i):
                freed(a, ("gate", 2 * KB - 1))
                a.activation(gsig[:, 4 * i:4 * i + 4, :], gsig[:, 4 * i:4 * i + 4, :], ACT.Sigmoid)\
                 .then_inc(gates_ready, 1)

            def copy_pT(h):
                job_done(a, ("pT", h))
                if h >= 4:
                    job_done(a, ("o", (h - 4) // 2))
                a.copy(pT[:, h % 4, :, :], bank[BANK_OF[("pT", h)]][:, 0:3 * P].rearrange(
                    "p (a n) -> p a n", a=3)).then_inc(act_evac, 1)

            def copy_o(b):
                job_done(a, ("o", b))
                a.copy(o_hi[:, b, :], bank[BANK_OF[("o", b)]][:, 0:T]).then_inc(o_hi_ready, 1)

            for b in range(AB):
                copy_pT(2 * b)
                copy_pT(2 * b + 1)
                if b:
                    copy_o(b - 1)
                if b == 1:
                    a.wait_ge(ln_out, 1)
                    for i in range(CB):
                        a.activation(acc[:, i, :], acc[:, i, :], ACT.Silu, bias=prm[:, C_LNB + i:C_LNB + i + 1],
                                     scale=prm[:, C_LNG + i:C_LNG + i + 1]).then_inc(silu, 1)
                if b == 2:
                    a.wait_ge(silu, CB)
                    a.copy(cu_hi[:, :, :], acc[:, :, :]).then_inc(cu_h, 1)
                if b in (3, 4):
                    gate_sigmoid(b - 3)
            copy_o(AB - 1)
            for n in range(T_CONV, T_ATT):
                split_hi(a, n + LEAD, 0, 0)
                if n < T_CONV + 2:
                    gate_sigmoid(2 + n - T_CONV)
            for b in range(KB):
                if T_ATT + b < T_MIX:
                    split_hi(a, T_ATT + b + LEAD, 0, 0)
                a.wait_ge(merged, b + 1)
                if b == 0:
                    job_done(a, ("gate", 2 * KB - 1))
                a.copy(nrm_hi[:, b, :], gsig[:, b, :]).then_inc(m_hi, 1)
            for b in range(KB):
                split_hi(a, T_MIX + b + LEAD, 0, 0)
                freed(a, ("mix", b))
                a.activation(sq[:, b, :], resid[:, b, :], ACT.Square).then_inc(squared, 1)
            job_done(a, ("ssq2",))
            a.activation(rs[:, 0, 0:T], bank[BANK_OF[("ssq2",)]][:, 0:T], ACT.Sqrt, bias=EPS, scale=1.0 / D)\
             .then_inc(act_evac, 1)
            for k in range(KB):
                split_norm(k, 1)
            for u in range(HALVES):
                split_hi(a, T_WQ + u + LEAD, 0, 0)
                job_done(a, ("wq", u))
                a.copy(qT[:, u, :], bank[BANK_OF[("wq", u)]][:, 0:T]).then_inc(act_evac, 1)
            for j in range(N_SC):
                a.wait_ge(sc_ready, j + 1)
                a.copy(S[:, 4 * j:4 * j + 4, :], bank[BANK_OF[("sc", j)]][:, :].rearrange(
                    "p (u n) -> p u n", n=NK)).then_inc(act_evac, 1)

            def gelu(base_i, it, j):
                a.wait_ge(pe_step, it * 4 + (S_U + base_i + j + 1))
                a.activation(act[:, it * 4 + (base_i + j), :], bank[4 + j % 2][:, 0:T], ACT.Gelu).then_inc(gelu_done, 1)

            a.preload_act_table(ACT.Gelu)
            with a.Fori(0, EXP_TILE // RING) as it:
                for j in range(RING):
                    split_hi(a, U0 + LEAD, it, j)
                    gelu(0, it, j)
            a.wait_ge(top_done, 1)
            a.activation(ex[:, :], ex[:, :], ACT.Exp).then_inc(gexp, 1)
            a.preload_act_table(ACT.Gelu)
            with a.Fori(EXP_TILE // RING, HALF // RING) as it:
                for j in range(RING):
                    split_hi(a, U0 + LEAD, it, j)
                    gelu(0, it, j)
            a.wait_ge(pick_ready, 2)
            with a.Fori(0, HALF // RING) as it:
                for j in range(RING):
                    split_hi(a, U0 + HALF + LEAD, it, j)
                    gelu(HALF, it, j)

            def a_split(base_i, it, j):
                wait(a, pe_step, it * 4 + (S_V + base_i + j - 3))
                a.copy(nrm_hi[:, (base_i + j) % RING, :], act[:, it * 4 + (base_i + j), :]).then_inc(a_hi, 1)

            a.wait_ge(pe_step, S_V)
            for half in range(2):
                a.wait_ge(gated, HALF * (half + 1))
                a_split(HALF * half, 0, 0)
                with a.Fori(0, HALF // RING - 1) as it:
                    for j in range(RING):
                        a_split(HALF * half + 1, it, j)
                        split_hi(a, V0 + HALF * half + LEAD, it, j)
                for j in range(RING):
                    if j < RING - 1:
                        a_split(HALF * (half + 1) - RING + 1, 0, j)
                    if half == 0 or j == 0:
                        split_hi(a, V0 + HALF * (half + 1) - RING + LEAD, 0, j)
            a.wait_ge(y_first, 1)
            a.copy(yout[:, 512:D], bank[1][:, :]).then_inc(y_act, 1)
            a.wait_ge(pe_step, S_V + N_V)
            a.copy(yout[:, D + 512:2 * D], bank[3][:, :]).then_inc(y_act, 1)

        @block.vector
        def _(dve):
            links = [0]

            def link(ins):
                links[0] += 1
                ins.then_inc(chain, 1)
                dve.wait_ge(chain, links[0])

            def lo_of(g):
                if by_dve(g, 0):
                    split_lo(dve, g, 0, 0)

            def normalise(gain, round_):
                def lower(k):
                    dve.wait_ge(nhi, KB * round_ + k + 1)
                    dve.tensor_tensor(nrm_lo[:, k, :], sq[:, k, :], nrm_hi[:, k, :].bitcast(F32), ALU.subtract)\
                       .then_inc(nlo, 1)

                link(dve.reciprocal(rs[:, 0, 0:T], rs[:, 0, 0:T]))
                for k in range(KB):
                    dve.scalar_tensor_tensor(out=sq[:, k, :], in0=resid[:, k, :], scalar=prm[:, gain + k:gain + k + 1],
                                             in1=rs[:, 0, 0:T], op0=ALU.mult, op1=ALU.mult).then_inc(normed, 1)
                    if k:
                        lower(k - 1)
                lower(KB - 1)

            dve.wait_ge(rel_in, 32)
            dve.wait_ge(const, 1)
            dve.tensor_copy(relb[:, :, :], relx[:, :].unsqueeze(2).broadcast_to([BUCKETS + 1, HEADS, P]))\
               .then_inc(relb_ready, 1)
            dve.wait_ge(prm_in, 16)
            dve.tensor_tensor(gains[:, :], prm[:, C_QG:C_QG + 1], prm[:, C_KG:C_KG + 1], ALU.mult).then_inc(gains_ready, 1)
            dve.wait_ge(x_in[0], 16)
            dve.wait_ge(x_in[1], 16)
            freed(dve, ("ssq1",))
            normalise(C_N1, 0)
            for g in range(LEAD):
                lo_of(g)

            def glu(b):
                job_done(dve, ("glu", 2 * b + 1))
                freed(dve, ("glu", 2 * b))
                dve.scalar_tensor_tensor(out=u_pad[:, b, TAPS - 1:], in0=bank[BANK_OF[("glu", 2 * b + 1)]][:, 0:T],
                                         scalar=prm[:, C_GLU + b:C_GLU + b + 1], in1=sig[:, b, :],
                                         op0=ALU.add, op1=ALU.mult).then_inc(dve_evac, 1)

            def conv_tap(w):
                for b in range(CB):
                    src = u_pad[:, b, w:w + T]
                    wt = prm[:, C_DW + b * TAPS + w:C_DW + b * TAPS + w + 1]
                    if w == 0:
                        dve.wait_ge(const, 4)
                        freed(dve, ("glu", 2 * b + 1))
                        dve.tensor_scalar(acc[:, b, :], src, wt, prm[:, C_DWB + b:C_DWB + b + 1], ALU.mult, ALU.add)\
                           .then_inc(tap, 1)
                    else:
                        dve.wait_ge(tap, CB * (w - 1) + b + 1)
                        dve.scalar_tensor_tensor(out=acc[:, b, :], in0=src, scalar=wt, in1=acc[:, b, :],
                                                 op0=ALU.mult, op1=ALU.add).then_inc(tap, 1)

            def k_norm(i):
                two = qk[:, AB + 2 * i:AB + 2 * i + 2, :].rearrange("p a t -> p (a t)")
                job_done(dve, ("kb", i))
                if i == 0:
                    dve.wait_ge(gains_ready, 1)
                dve.scalar_tensor_tensor(out=two, in0=two, scalar=gains[:, 0:1], in1=bank[BANK_OF[("kb", i)]][:, :],
                                         op0=ALU.mult, op1=ALU.mult).then_inc(dve_evac, 1)

            def score(s):
                c, pair = divmod(s, len(PAIRS))
                h0 = PAIRS[pair][0]
                w = P * (c + 1)
                job_done(dve, ("score", s))
                for r, h in enumerate(PAIRS[pair]):
                    col = c * HEADS + h
                    ins = dve.scalar_tensor_tensor(out=p3[:, h, c * P:c * P + w],
                                                   in0=bank[BANK_OF[("score", s)]][:, r * w:(r + 1) * w],
                                                   scalar=rq[:, col:col + 1], in1=bias[:, h, T - w:T],
                                                   op0=ALU.mult, op1=ALU.add)
                    ins.then_inc(dve_evac if r else biased, 1)
                freed(dve, ("score", s))
                dve.wait_ge(biased, s + 1)
                dve.tensor_reduce(negm[:, c * HEADS + h0:c * HEADS + h0 + 3:2], p3[:, h0:h0 + 3:2, c * P:c * P + w],
                                  AX.X, ALU.max, negate=True).then_inc(score_max, 1)

            def group_weights():
                dve.wait_ge(lns, 1)
                link(dve.tensor_tensor(lse[:, :], lnl[:, :], negm[:, :], ALU.subtract))
                lse4 = lse[:, :].rearrange("p (c g s) -> p c s g", c=TC, g=GROUPS)
                for c in range(TC):
                    link(dve.tensor_reduce(gmax[:, c * SLOTS:(c + 1) * SLOTS], lse4[:, c], AX.X, ALU.max))
                for c in range(TC):
                    l3 = lse[:, c * HEADS:(c + 1) * HEADS].rearrange("p (g s) -> p g s", g=GROUPS)
                    m3 = gmax[:, c * SLOTS:(c + 1) * SLOTS].unsqueeze(1).broadcast_to([P, GROUPS, SLOTS])
                    dve.tensor_tensor(l3, l3, m3, ALU.subtract).then_inc(wexp, 1)

            def group_factors():
                dve.wait_ge(lns, 2)
                ew4 = ew[:, :].rearrange("p (c g s) -> p c s g", c=TC, g=GROUPS)
                for c in range(TC):
                    link(dve.tensor_reduce(gsum[:, c * SLOTS:(c + 1) * SLOTS], ew4[:, c], AX.X, ALU.add))
                for c in range(TC):
                    z3 = zz[:, c * HEADS:(c + 1) * HEADS].rearrange("p (g s) -> p g s", g=GROUPS)
                    l3 = lsum[:, c * HEADS:(c + 1) * HEADS].rearrange("p (g s) -> p g s", g=GROUPS)
                    g3 = gsum[:, c * SLOTS:(c + 1) * SLOTS].unsqueeze(1).broadcast_to([P, GROUPS, SLOTS])
                    link(dve.tensor_tensor(z3, l3, g3, ALU.mult))
                link(dve.reciprocal(fac[:, :], zz[:, :]))
                link(dve.tensor_tensor(fac[:, :], fac[:, :], ew[:, :], ALU.mult))

            def scale_probs(h):
                for c in range(TC):
                    pr = p3[:, h, c * P:(c + 1) * P + c * P]
                    col = c * HEADS + h
                    dve.tensor_scalar(pr, pr, fac[:, col:col + 1], None, ALU.mult).then_inc(scaled, 1)

            for n in range(T_CONV):
                lo_of(n + LEAD)
                if n < T_QK and n % 2:
                    glu(n // 2)
                for w_ in TAPS_AT.get(n, ()):
                    conv_tap(w_)
                if n == 3:
                    dve.wait_ge(const, 8)
                    dve.tensor_copy(ksel[:, :, :].rearrange("p b (r d) -> p b r d", r=2),
                                    ident[0:HEADS, 0:HEADS].rearrange("p (b r) -> p b r", r=2).unsqueeze(3)
                                    .broadcast_to([HEADS, AB, 2, HD])).then_inc(rk_ready, 1)
                if n == QSS_AT + 1:
                    freed(dve, ("qss",))
                    dve.reciprocal(rq[:, :], rq[:, :]).then_inc(rq_ready, 1)
                if n == KSS_AT + 1:
                    freed(dve, ("kss",))
                    dve.reciprocal(rk, rk).then_inc(rk_ready, 1)
                if n == KB_AT + 1:
                    for i in range(AB // 2):
                        k_norm(i)
                if n == min(SCORES_AT) + 1:
                    dve.wait_ge(bias_in, 16 * HEADS)
                    dve.wait_ge(rq_ready, 1)
                for i in SCORES_AT.get(n - 1, ()):
                    score(i)
                if n == WEIGHTS_AT + 1:
                    group_weights()
                if n == LNSUM_AT + 1:
                    job_done(dve, ("lnsum",))
                    dve.wait_ge(tap, CB * TAPS)
                    dve.tensor_scalar(rs[:, 1, 0:T], bank[BANK_OF[("lnsum",)]][:, 0:T], 1.0 / CONV_CH, None, ALU.mult)\
                       .then_inc(dve_evac, 1)
                    freed(dve, ("lnsum",))
                    dve.tensor_tensor(u_pad[:, :, 0:T], acc[:, :, :], rs[:, 1:2, 0:T].broadcast_to([P, CB, T]),
                                      ALU.subtract).then_inc(centred, 1)
                    group_factors()
                if n > LNSUM_AT + 1:
                    for h in range(4 * (n - LNSUM_AT - 2), min(HEADS, 4 * (n - LNSUM_AT - 1))):
                        scale_probs(h)
            freed(dve, ("lnvar",))
            link(dve.reciprocal(rs[:, 0, 0:T], rs[:, 0, 0:T]))
            dve.tensor_tensor(acc[:, :, :], u_pad[:, :, 0:T], rs[:, 0:1, 0:T].broadcast_to([P, CB, T]), ALU.mult)\
               .then_inc(ln_out, 1)
            for b in range(AB):
                if b == 2:
                    dve.wait_ge(cu_h, 1)
                    dve.tensor_tensor(cu_lo[:, :, :], acc[:, :, :], cu_hi[:, :, :].bitcast(F32), ALU.subtract)\
                       .then_inc(cu_l, 1)
                dve.wait_ge(o_hi_ready, b + 1)
                dve.tensor_tensor(o_lo[:, b, :], bank[BANK_OF[("o", b)]][:, 0:T], o_hi[:, b, :].bitcast(F32),
                                  ALU.subtract).then_inc(dve_evac, 1)
            for b in range(KB):
                if b % 2 == 0:
                    lo_of(T_CONV + b // 2 + LEAD)
                job_done(dve, ("conv", b))
                dve.wait_ge(gates_ready, b // 4 + 1)
                dve.scalar_tensor_tensor(out=gsig[:, b, :], in0=bank[BANK_OF[("conv", b)]][:, 0:T],
                                         scalar=prm[:, C_BP + b:C_BP + b + 1], in1=gsig[:, b, :],
                                         op0=ALU.add, op1=ALU.mult).then_inc(dve_evac, 1)
            for b in range(KB):
                dve.wait_ge(gates_ready, 2 + b // 4 + 1)
                if T_ATT + b < T_MIX:
                    lo_of(T_ATT + b + LEAD)
                job_done(dve, ("attn", b))
                dve.tensor_tensor(gsig[:, KB + b, :], bank[BANK_OF[("attn", b)]][:, 0:T], gsig[:, KB + b, :],
                                  ALU.mult).then_inc(dve_evac, 1)
                freed(dve, ("attn", b))
                dve.tensor_tensor(gsig[:, b, :], gsig[:, b, :], gsig[:, KB + b, :], ALU.add).then_inc(merged, 1)
                dve.wait_ge(m_hi, b + 1)
                dve.wait_ge(merged, b + 1)
                dve.tensor_tensor(nrm_lo[:, b, :], gsig[:, b, :], nrm_hi[:, b, :].bitcast(F32), ALU.subtract)\
                   .then_inc(m_lo, 1)
            for b in range(KB):
                lo_of(T_MIX + b + LEAD)
                job_done(dve, ("mix", b))
                dve.tensor_tensor(resid[:, b, :], bank[BANK_OF[("mix", b)]][:, 0:T], resid[:, b, :], ALU.add)\
                   .then_inc(dve_evac, 1)
            freed(dve, ("ssq2",))
            dve.wait_ge(dve_evac, FREED[("mix", KB - 1)])
            normalise(C_N2, 1)
            for u in range(HALVES):
                lo_of(T_WQ + u + LEAD)

            dve.wait_ge(const, 9)

            def top16(pair):
                ended = [0, 0]
                for stage in range(5):
                    for r, (vals, idx, row) in enumerate(pair):
                        if stage:
                            dve.wait_ge(chain, ended[r])
                        if stage in (0, 3):
                            ins = dve.max(vals[:, 8 * (stage // 3):8 * (stage // 3) + 8], row)
                        elif stage == 2:
                            ins = dve.match_replace(row, vals[:, 0:8], row, LOWEST)
                        else:
                            f = 8 * (stage // 4)
                            ins = dve.max_index(idx[:, f:f + 8], vals[:, f:f + 8], row)
                        links[0] += 1
                        ended[r] = links[0]
                        ins.then_inc(chain, 1)
                dve.wait_ge(chain, links[0])

            def candidates(c):
                t3 = topv[:, c * HALVES:(c + 1) * HALVES, :]
                link(dve.tensor_tensor(cand[:, :, :].rearrange("p h (a b) -> p h a b", a=TOPK),
                                       t3[:, 0::2, :].unsqueeze(3).broadcast_to([P, PH, TOPK, TOPK]),
                                       t3[:, 1::2, :].unsqueeze(2).broadcast_to([P, PH, TOPK, TOPK]), ALU.add))

            def lookup(c, w, stage):
                pos = (cf1, cf2)[w][:, c * P:(c + 1) * P]
                e4 = eq[:, :].rearrange("p (h k j) -> p h k j", h=PH, k=TOPK)
                e3 = eq[:, :].rearrange("p (n j) -> p n j", j=TOPK)
                if stage == 0:
                    link(dve.tensor_tensor(e3, pos.unsqueeze(2).broadcast_to([P, PH * TOPK, TOPK]),
                                           iota[:, 0:TOPK].unsqueeze(1).broadcast_to([P, PH * TOPK, TOPK]),
                                           ALU.is_equal))
                elif stage == 1:
                    tf = topf[:, c * HALVES + w:(c + 1) * HALVES:2, :].unsqueeze(2).broadcast_to([P, PH, TOPK, TOPK])
                    link(dve.tensor_tensor(e4, e4, tf, ALU.mult))
                else:
                    link(dve.tensor_reduce(sel[:, w, c, :], e3, AX.X, ALU.add))

            def top_step(i):
                if i < HALVES:
                    if i % 2 == 0:
                        freed(dve, ("sc", i // 2))
                    top16([(topv[:, u, :], topi[:, u, :], S[:, u, :]) for u in (2 * i, 2 * i + 1)])
                elif i == HALVES:
                    link(dve.tensor_copy(topf[:, :, :], topi[:, :, :]))
                else:
                    c, r = divmod(i - HALVES - 1, CHUNK_STEPS)
                    both = slice(c * P, (c + 1) * P)
                    if r == 0:
                        candidates(c)
                    elif r <= PH // 2:
                        heads = (2 * r - 2, 2 * r - 1)
                        top16([(bestv[:, c * PH + h, :], besti[:, (c * PH + h) * TOPK:(c * PH + h + 1) * TOPK],
                                cand[:, h, :]) for h in heads])
                    elif r == PH // 2 + 1:
                        link(dve.tensor_scalar(bc1[:, both], besti[:, both], 4, None, ALU.logical_shift_right))
                        link(dve.tensor_scalar(bc2[:, both], besti[:, both], 15, None, ALU.bitwise_and))
                        link(dve.tensor_copy(cf1[:, both], bc1[:, both]))
                        link(dve.tensor_copy(cf2[:, both], bc2[:, both]))
                    elif r < PH // 2 + 8:
                        lookup(c, *divmod(r - PH // 2 - 2, 3))
                    else:
                        b3 = bestv[:, c * PH:(c + 1) * PH, :]
                        x3 = ex[:, both].rearrange("p (u k) -> p u k", k=TOPK)
                        ins = dve.tensor_tensor(x3, b3, b3[:, :, 0:1].broadcast_to([P, PH, TOPK]), ALU.subtract)
                        if c:
                            ins.then_inc(top_done, 1)
                        else:
                            link(ins)

            def softmax_gates():
                dve.wait_ge(gexp, 1)
                e3 = ex[:, :].rearrange("p (u k) -> p u k", k=TOPK)
                link(dve.tensor_reduce(zs[:, 0, :], e3, AX.X, ALU.add))
                link(dve.reciprocal(zs[:, 1, :], zs[:, 0, :]))
                dve.tensor_tensor(gate[:, :, :].rearrange("p c (u k) -> p (c u) k", k=TOPK), e3,
                                  zs[:, 1, :].unsqueeze(2).broadcast_to([P, TC * PH, TOPK]), ALU.mult)\
                   .then_inc(gate_ready, 1)

            weights = [21] * HALVES + [10] + TC * ([23] + [35] * (PH // 2) + [8] + [23] * 6 + [3])
            tile_of = [int(TOP_TILES * sum(weights[:n]) / sum(weights)) for n in range(len(weights))]
            for i in range(HALF):
                if by_dve(U0 + LEAD, i):
                    split_lo(dve, U0 + LEAD, 0, i)
                for n, tile in enumerate(tile_of):
                    if tile == i:
                        top_step(n)
                if i == EXP_TILE + 2:
                    softmax_gates()
            dve.wait_ge(pick_T, 1)
            dve.tensor_copy(keys[:, :, :], bank[6][:, :].rearrange("p (a t) -> p a t", a=2)).then_inc(pick_ready, 1)
            dve.wait_ge(pick_T, 2)
            link(dve.tensor_copy(pickf[:, 0, :], bank[7][:, 0:T]))
            link(dve.tensor_copy(parts[:, 0, :], pickf[:, 0, :]))
            link(dve.tensor_tensor(pickf[:, 1, :], pickf[:, 0, :], parts[:, 0, :], ALU.subtract))
            link(dve.tensor_copy(parts[:, 1, :], pickf[:, 1, :]))
            dve.tensor_tensor(parts[:, 2, :], pickf[:, 1, :], parts[:, 1, :], ALU.subtract).then_inc(pick_ready, 1)
            dve.wait_ge(pick_ready, 2)
            dve.wait_ge(const, 10)

            def one_hots(half, it, j):
                n = it * 4 + (half * HALF + j)
                t = bass.ds(it * (4 * TOK) + j * TOK, TOK)
                wait(dve, gate_mm, n - 1)

                def at(x, m):
                    return x.unsqueeze(1).broadcast_to([P, m, TOK])

                dve.tensor_tensor(eqB[:, j % 2], iota4[:, half * HALF:(half + 1) * HALF, :], at(keys[:, 1, t], HALF),
                                  ALU.is_equal).then_inc(second, 1)
                dve.tensor_tensor(ohA[:, j % 2], iota4[:, :, :], at(keys[:, 0, t], NK), ALU.is_equal)\
                   .then_inc(spread, 1)
                dve.wait_ge(second, n + 1)
                dve.tensor_tensor(ohB[:, j % 2], eqB[:, j % 2].unsqueeze(1).broadcast_to([P, 3, HALF, TOK]),
                                  parts[:, :, t].unsqueeze(2).broadcast_to([P, 3, HALF, TOK]), ALU.mult)\
                   .then_inc(spread, 1)

            def multiply(half, it, j):
                n = it * 4 + (half * HALF + j)
                wait(dve, gate_mm, n + 1)
                av = act[:, half * HALF:(half + 1) * HALF, bass.ds(it * (4 * TOK) + j * TOK, TOK)]
                gv = bank[6 + j % 2][:, 0:TOK * HALF].rearrange("p (q n) -> p n q", q=TOK)
                dve.tensor_tensor(av, av, gv, ALU.mult).then_inc(gated, 1)

            def low_part(base_i, it, j):
                dve.wait_ge(a_hi, it * 4 + (base_i + j + 1))
                s = (base_i + j) % RING
                dve.tensor_tensor(nrm_lo[:, s, :], act[:, it * 4 + (base_i + j), :], nrm_hi[:, s, :].bitcast(F32),
                                  ALU.subtract).then_inc(a_lo, 1)

            def gate_body(half, it, first=False, last=False):
                base = U0 + HALF if half == 0 else V0
                for j in range(RING):
                    if half == 1 and not (last and j == RING - 1):
                        low_part(1, it, j)
                    if not (last and j == RING - 1):
                        one_hots(half, it, j + 1)
                    if first and j == 0:
                        dve.wait_ge(gelu_done, HALF * (half + 1))
                    multiply(half, it, j)
                    if by_dve(base + LEAD, j):
                        split_lo(dve, base + LEAD, it, j)

            for half in range(2):
                one_hots(half, 0, 0)
                if half == 1:
                    low_part(0, 0, 0)
                gate_body(half, 0, first=True)
                with dve.Fori(1, HALF // RING - 1) as it:
                    gate_body(half, it)
                gate_body(half, HALF // RING - 1, last=True)
            low_part(HALF, 0, 0)
            with dve.Fori(0, HALF // RING - 1) as it:
                for j in range(RING):
                    low_part(HALF + 1, it, j)
                    if by_dve(V0 + HALF + LEAD, j):
                        split_lo(dve, V0 + HALF + LEAD, it, j)
            for j in range(RING - 1):
                low_part(N_V - RING + 1, 0, j)
                if j == 0:
                    split_lo(dve, V0 + N_V - 1, 0, 0)
            dve.wait_ge(y_first, 1)
            dve.tensor_copy(yout[:, 0:512], bank[0][:, :]).then_inc(y_dve, 1)
            dve.wait_ge(pe_step, S_V + N_V)
            dve.tensor_copy(yout[:, D:D + 512], bank[2][:, :]).then_inc(y_dve, 1)

        @block.tensor
        def _(pe):
            done = [0]

            def step(ins):
                done[0] += 1
                ins.then_inc(pe_step, 1)

            def start(job):
                i = JOBS.index(job)
                if i >= 8:
                    freed(pe, JOBS[i - 8])
                return bank[BANK_OF[job]]

            def product(dst, s, units, vec_hi, vec_lo, base, it, j, first=True, last=True):
                wait_lo(pe, base, it, j)
                n = len(units)
                for i, (u, k) in enumerate(units):
                    for p_, (w_, x_) in enumerate(((hi, vec_hi), (hi, vec_lo), (lo, vec_hi))):
                        ins = pe.matmul(dst, w_[:, s, u * P:(u + 1) * P], x_[:, k, :],
                                        start=first and i == 0 and p_ == 0, stop=last and i == n - 1 and p_ == 2)
                return ins

            def full(n, job):
                b = start(job)
                return product(b[:, 0:T], n % RING, [(k, k) for k in range(KB)], nrm_hi, nrm_lo, n, 0, 0)

            def bias_row(h):
                b = start(("bias", h))
                step(pe.matmul(b[:, 0:BW], relb[:, h, :], oneh[:, h // SLOTS, :], start=True, stop=True))

            pe.wait_ge(relb_ready, 1)
            pe.wait_ge(rel_in, 32)
            bias_row(0)
            bias_row(1)
            pe.wait_ge(const, 7)
            b = start(("ssq1",))
            for k in range(KB):
                pe.wait_ge(squared, k // 4 + 1)
                ins = pe.matmul(b[:, 0:T], ones[:, :], sq[:, k, :], start=k == 0, stop=k == KB - 1)
            step(ins)
            for h in range(2, 7):
                bias_row(h)

            def two_tiles(jobs, tiles, parts_ready):
                banks = [start(job) for job in jobs]
                for k in range(KB):
                    parts_ready(k)
                    for b, n in zip(banks, tiles):
                        ins = product(b[:, 0:T], n % RING, [(k, k)], nrm_hi, nrm_lo, n, 0, 0,
                                      first=k == 0, last=k == KB - 1)
                        if k == KB - 1:
                            step(ins)

            def norm_ready(round_):
                def wait_k(k):
                    pe.wait_ge(nlo, KB * round_ + k + 1)
                return wait_k

            def q_sums():
                b = start(("qss",))
                pe.wait_ge(qk_sq, AB)
                for c in range(TC):
                    for i in range(AB):
                        col = c * HEADS + 2 * i
                        ins = pe.matmul(b[:, col:col + 2], sq[:, i, c * P:(c + 1) * P], kmask[:, HEADS - 2:HEADS],
                                        start=c == 0 and i == 0, stop=True, skip_group_check=True)
                step(ins)

            def k_sums():
                b = start(("kss",))
                pe.wait_ge(qk_sq, 2 * AB)
                for i in range(AB):
                    ins = pe.matmul(b[0:HEADS, 0:T], kmask[:, HEADS - 2 - 2 * i:2 * HEADS - 2 - 2 * i],
                                    sq[:, (AB + i) % KB, :], start=i == 0, stop=i == AB - 1)
                step(ins)

            def spread_k(i):
                b = start(("kb", i))
                pe.wait_ge(rk_ready, 2)
                for r in range(2):
                    ins = pe.matmul(b[:, r * T:(r + 1) * T], ksel[:, 2 * i + r, :], rk,
                                    start=r == 0, stop=True, skip_group_check=True)
                step(ins)

            def turn_v(i):
                b = start(("vt", i))
                pe.wait_ge(const, 8)
                for r in range(2):
                    freed(pe, ("v", 2 * i + r))
                    for c in range(TC):
                        ins = pe.transpose(b[:, (2 * r + c) * P:(2 * r + c + 1) * P],
                                           vT[:, (2 * i + r) % CB, c * P:(c + 1) * P], ident[:, :])
                step(ins)

            def scores(s):
                c, pair = divmod(s, len(PAIRS))
                w = P * (c + 1)
                b = start(("score", s))
                freed(pe, ("kb", AB // 2 - 1))
                for r, h in enumerate(PAIRS[pair]):
                    rows = slice((h % 2) * HD, (h % 2 + 1) * HD)
                    ins = pe.matmul(b[:, r * w:(r + 1) * w], qk[rows, h // 2, c * P:(c + 1) * P],
                                    qk[rows, AB + h // 2, 0:w], start=r == 0, stop=True, skip_group_check=True)
                step(ins)

            for n in range(T_CONV):
                if n == 0:
                    two_tiles([("glu", 0), ("glu", 1)], [0, 1], norm_ready(0))
                elif n == 1:
                    pass
                elif n < T_QK:
                    step(full(n, ("glu", n)))
                elif n < T_V:
                    step(full(n, ("qk", n - T_QK)))
                elif n < T_GATE:
                    step(full(n, ("v", n - T_V)))
                else:
                    step(full(n, ("gate", n - T_GATE)))
                for h in BIAS_AT.get(n, ()):
                    bias_row(h)
                if n == QSS_AT:
                    q_sums()
                if n == KSS_AT:
                    k_sums()
                if n == KB_AT:
                    for i in range(AB // 2):
                        spread_k(i)
                if n in VT_AT:
                    turn_v(VT_AT[n])
                for i in SCORES_AT.get(n, ()):
                    scores(i)
                if n == LNSUM_AT:
                    b = start(("lnsum",))
                    pe.wait_ge(tap, CB * TAPS)
                    for k in range(CB):
                        ins = pe.matmul(b[:, 0:T], ones[:, :], acc[:, k, :], start=k == 0, stop=k == CB - 1)
                    step(ins)
                if n == LNVAR_AT:
                    b = start(("lnvar",))
                    pe.wait_ge(centred_sq, 1)
                    for k in range(CB):
                        ins = pe.matmul(b[:, 0:T], ones[:, :], sq[:, k, :], start=k == 0, stop=k == CB - 1)
                    step(ins)

            def turn(h):
                b = start(("pT", h))
                pe.wait_ge(scaled, 2 * h + 2)
                pe.wait_ge(const, 8)
                for r in range(3):
                    ins = pe.transpose(b[:, r * P:(r + 1) * P], p3[:, h, r * P:(r + 1) * P], ident[:, :])
                step(ins)

            freed(pe, ("vt", AB // 2 - 1))

            def attend(bl):
                b = start(("o", bl))
                for r in range(2):
                    h = 2 * bl + r
                    freed(pe, ("pT", h))
                    dst = b[r * HD:(r + 1) * HD, 0:T]
                    vv = [v[:, c, h * HD:(h + 1) * HD] for c in range(TC)]
                    pe.matmul(dst[:, 0:P], vv[0], pT[:, h % 4, 0, :], start=True, stop=True, skip_group_check=True)
                    pe.matmul(dst[:, P:T], vv[0], pT[:, h % 4, 1, :], start=True, stop=False, skip_group_check=True)
                    ins = pe.matmul(dst[:, P:T], vv[1], pT[:, h % 4, 2, :], start=False, stop=True,
                                    skip_group_check=True)
                step(ins)

            for bl in range(AB):
                turn(2 * bl)
                turn(2 * bl + 1)
                if bl:
                    attend(bl - 1)
            attend(AB - 1)
            pe.wait_ge(cu_l, 1)
            for b_ in range(KB):
                n = T_CONV + b_ // 2
                b = start(("conv", b_))
                step(product(b[:, 0:T], n % RING, [((b_ % 2) * CB + k, k) for k in range(CB)], cu_hi, cu_lo, n, 0, 0))
            freed(pe, ("o", AB - 1))
            for b_ in range(KB):
                b = start(("attn", b_))
                units = list(range(AB * b_, AB * b_ + AB))
                for tile in sorted({u // 8 for u in units}):
                    mine = [u for u in units if u // 8 == tile]
                    n = T_ATT + tile
                    ins = product(b[:, 0:T], n % RING, [(u % 8, u % AB) for u in mine], o_hi, o_lo, n, 0, 0,
                                  first=mine[0] == units[0], last=mine[-1] == units[-1])
                    if mine[-1] == units[-1] or mine[-1] % 8 == 7:
                        step(ins)
            two_tiles([("mix", 0), ("mix", 1)], [T_MIX, T_MIX + 1], lambda k: pe.wait_ge(m_lo, k + 1))
            for b_ in range(2, KB):
                step(full(T_MIX + b_, ("mix", b_)))
            b = start(("ssq2",))
            for k in range(KB):
                pe.wait_ge(squared, 2 + k + 1)
                ins = pe.matmul(b[:, 0:T], ones[:, :], sq[:, k, :], start=k == 0, stop=k == KB - 1)
            step(ins)
            two_tiles([("wq", 0), ("wq", 1)], [T_WQ, T_WQ + 1], norm_ready(1))
            for u in range(2, HALVES):
                step(full(T_WQ + u, ("wq", u)))
            assert done[0] == FRONT_STEPS
            pe.wait_ge(sk_in, 16)
            for j in range(N_SC):
                b = start(("sc", j))
                for r in range(4):
                    c, u = divmod(4 * j + r, HALVES)
                    freed(pe, ("wq", u))
                    ins = pe.matmul(b[:, r * NK:(r + 1) * NK], qT[:, u, c * P:(c + 1) * P], skT[:, u, :],
                                    start=r == 0, stop=True, skip_group_check=True)
                ins.then_inc(sc_ready, 1)
            for j in range(N_SC):
                freed(pe, ("sc", j))

            for c in range(TC):
                for k in range(KB):
                    ins = pe.matmul(bank[2 * c + k // 4][:, (k % 4) * P:(k % 4 + 1) * P], resid[:, k, c * P:(c + 1) * P],
                              ident[:, :], start=k % 4 == 0, stop=False, skip_group_check=True)
            ins.then_inc(y_began, 1)

            def u_tile(base_i, it, j):
                wait(pe, gelu_done, it * 4 + (base_i + j - 1))
                ins = product(bank[4 + j % 2][:, 0:T], j, [(k, k) for k in range(KB)], nrm_hi, nrm_lo, U0 + base_i, it, j)
                ins.then_inc(pe_step, 1)

            def gates(half, it, j):
                n = it * 4 + (half * HALF + j)
                wait(pe, gated, n - 1)
                pe.wait_ge(spread, n * 2 + 2)
                for q in range(TOK):
                    for i in range(3):
                        ins = pe.matmul(bank[6 + j % 2][:, q * HALF:(q + 1) * HALF], ohA[:, j % 2, :, q],
                                        ohB[:, j % 2, i, :, q], start=i == 0, stop=i == 2, skip_group_check=True)
                ins.then_inc(gate_mm, 1)

            for j in range(RING):
                u_tile(0, 0, j)
            with pe.Fori(1, PICK_TILE // RING) as it:
                for j in range(RING):
                    u_tile(0, it, j)
            pe.wait_ge(top_done, 1)
            for w in range(2):
                for c in range(TC):
                    ins = pe.transpose(bank[6][:, w * T + c * P:w * T + (c + 1) * P], sel[:, w, c, :], ident[:, :])
            ins.then_inc(pick_T, 1)
            pe.wait_ge(gate_ready, 1)
            for c in range(TC):
                ins = pe.transpose(bank[7][:, c * P:(c + 1) * P], gate[:, c, :], ident[:, :])
            ins.then_inc(pick_T, 1)
            with pe.Fori(PICK_TILE // RING, HALF // RING) as it:
                for j in range(RING):
                    u_tile(0, it, j)

            def u_and_gates(it):
                for j in range(RING):
                    gates(0, it, j)
                    u_tile(HALF, it, j)

            u_and_gates(0)
            with pe.Fori(1, HALF // RING) as it:
                u_and_gates(it)

            def v_tile(base_i, it, j, stop=False):
                wait_lo(pe, V0 + base_i, it, j)
                pe.wait_ge(a_hi, it * 4 + (base_i + j + 1))
                for c in range(TC):
                    for a_, v_ in ((nrm_hi, hi), (nrm_hi, lo), (nrm_lo, hi)):
                        if c == 0 and a_ is nrm_lo:
                            pe.wait_ge(a_lo, it * 4 + (base_i + j + 1))
                        for half in range(2):
                            ins = pe.matmul(bank[2 * c + half][:, :], a_[:, j, c * P:(c + 1) * P],
                                            v_[:, j, half * 512:(half + 1) * 512],
                                            start=False, stop=stop and a_ is nrm_lo, skip_group_check=True)
                    if stop and c == 0:
                        ins.then_inc(y_first, 1)
                ins.then_inc(pe_step, 1)

            def v_and_gates(it):
                for j in range(RING):
                    gates(1, it, j)
                    v_tile(0, it, j)

            v_and_gates(0)
            with pe.Fori(1, HALF // RING) as it:
                v_and_gates(it)
            with pe.Fori(0, HALF // RING - 1) as it:
                for j in range(RING):
                    v_tile(HALF, it, j)
            for j in range(RING):
                v_tile(N_V - RING, 0, j, stop=j == RING - 1)


def bucket_rows():
    n = 255 - np.arange(BW)
    exact = BUCKETS // 2
    nf = np.maximum(n, 1).astype(np.float32)
    large = exact + (np.log(nf / np.float32(exact)) / np.float32(np.log(MAX_DISTANCE / exact))
                     * np.float32(BUCKETS - exact)).astype(np.int32)
    bucket = np.where(n < exact, n, np.minimum(large, BUCKETS - 1))
    rows = np.zeros((BUCKETS + 1, GROUPS, BW), np.float32)
    for g, (window, dilation) in enumerate(WINDOWS):
        valid = (n >= 0) & (n <= window) & (n % dilation == 0)
        rows[np.where(valid, bucket, BUCKETS), g, np.arange(BW)] = 1.0
    return rows


def kernel(**inputs):
    from concourse.bacc import Bacc
    from concourse.bass_utils import run_bass_kernel_spmd

    a = {k: np.asarray(x) for k, x in inputs.items()}

    def tiles(w, blocks):
        k = w.shape[0] // P
        return w.reshape(k, P, -1, P).transpose(2, 0, 1, 3)[blocks].reshape(-1, 8, P, P)\
                .transpose(0, 2, 1, 3).reshape(-1, P, 8 * P)

    glu = [b for pair in zip(range(CB, 2 * CB), range(CB)) for b in pair]
    n_in = a["w_in"].shape[2] // P
    front = np.concatenate([
        tiles(a["w_in"][0], glu + list(range(2 * CB, n_in))),
        tiles(a["conv_w_proj"][0], list(range(KB))),
        tiles(a["attn_w_proj"][0], list(range(KB))),
        tiles(a["mix_w_out"][0], list(range(KB))),
        tiles(a["peer_w_q"][0], list(range(HALVES))),
    ])

    def col(x):
        return x.reshape(-1, P).T

    cols = np.concatenate([
        col(a["norm1_g"][0]), col(a["norm2_g"][0]), col(a["conv_b_glu"][0]),
        a["conv_dw_w"][0, :, 0].reshape(TAPS, CB, P).transpose(2, 1, 0).reshape(P, CB * TAPS),
        col(a["conv_dw_b"][0]), col(a["conv_ln_g"][0]), col(a["conv_ln_b"][0]), col(a["conv_b_proj"][0]),
        np.tile(a["q_norm_g"][0], 2)[:, None], np.tile(a["k_norm_g"][0], 2)[:, None],
    ], axis=1)
    arrays = {
        "x_t": a["x"][0].T.reshape(KB, P, T).transpose(1, 0, 2),
        "front": front,
        "cols": cols,
        "rel_bias": a["rel_bias"],
        "onehot": bucket_rows(),
        "sub_keys": a["peer_sub_keys"][0].reshape(HALVES, NK, P).transpose(2, 0, 1),
        "u_tiles": a["peer_u"][0].reshape(NK, NK, KB, P).transpose(1, 3, 2, 0).reshape(NK, P, D),
        "v_tiles": a["peer_v"][0].reshape(NK, NK, D).transpose(1, 0, 2),
    }
    arrays = {k: np.ascontiguousarray(x) for k, x in arrays.items()}
    nc = Bacc("TRN2", target_bir_lowering=False, num_devices=1)
    args = [nc.dram_tensor(k, x.shape, mybir.dt.from_np(x.dtype), kind="ExternalInput").ap()
            for k, x in arrays.items()]
    y = nc.dram_tensor("y", (TC, P, D), F32, kind="ExternalOutput").ap()
    hybrid_block(nc, *args, y)
    r = run_bass_kernel_spmd(nc, [arrays], core_ids=[0])
    return r.results[0]["y"].reshape(1, T, D)
```

```python
from contextlib import ExitStack

import numpy as np

import concourse.bass as bass
from concourse import mybir

F32 = mybir.dt.float32
F32R = mybir.dt.float32r
U32 = mybir.dt.uint32
F16 = mybir.dt.float16
ALU = mybir.AluOpType
ACT = mybir.ActivationFunctionType
AX = mybir.AxisListType

P = 128
D = 1024
T = 256
KB = D // P
TC = T // P
CONV_CH, TAPS = 512, 31
CB = CONV_CH // P
HEADS, HD = 12, 64
SLOTS, GROUPS = 4, 3
AW = HEADS * HD
AB = AW // P
WINDOWS = ((128, 1), (512, 4), (2048, 16))
BUCKETS, MAX_DISTANCE = 32, 2048
PH, NK, TOPK = 8, 128, 16
HALVES = 2 * PH
EPS = 1e-6
NEG = -1e30
LOWEST = -3.0e38
BW = 384

T_GLU, T_QK, T_V, T_GATE = 0, 8, 20, 26
T_CONV, T_ATT, T_MIX, T_WQ = 42, 46, 52, 60
N_FRONT = 76
N_U = N_V = NK
RING = 4
LEAD = 3
CHUNK_STEPS = PH // 2 + 9
TOP_TILES = 48
EXP_TILE = 52
PICK_TILE = 60
HALF = NK // 2
GATE_SCALE = 2.0 ** 15
WARM_UP = 12
G_SHARED = N_FRONT + HALF + LEAD
TOK = 8
GROUPS_N = T // TOK

BIAS_AT = {1: (7, 8, 9), 2: (10, 11)}
QSS_AT, KSS_AT, KB_AT = 15, 20, 22
SCORES_AT = {24: (0, 1), 25: (2, 3), 26: (4, 5), 27: (6,), 28: (7,), 29: (8,), 30: (9,), 31: (10,), 32: (11,)}
LNSUM_AT, LNVAR_AT = 37, 40
WEIGHTS_AT = 35
TAPS_AT = {}
for _w in range(TAPS):
    TAPS_AT.setdefault(T_QK + (_w * 4 // 5 if _w < 18 else 14 + _w - 17), []).append(_w)


def jobs_in_order():
    order = [(("ssq1",), None)] + [(("bias", h), None) for h in range(7)]
    for n in range(T_CONV):
        if n < T_QK:
            order.append((("glu", n), n))
        elif n < T_V:
            order.append((("qk", n - T_QK), n))
        elif n < T_GATE:
            order.append((("v", (n - T_V) // 2) if (n - T_V) % 2 else None, n))
        else:
            order.append((("gate", n - T_GATE), n))
        order += [(("bias", h), None) for h in BIAS_AT.get(n, ())]
        if n == QSS_AT:
            order.append((("qss",), None))
        if n == KSS_AT:
            order.append((("kss",), None))
        if n == KB_AT:
            order += [(("kb", i), None) for i in range(AB // 2)]
        order += [(("score", i), None) for i in SCORES_AT.get(n, ())]
        if n == LNSUM_AT:
            order.append((("lnsum",), None))
        if n == LNVAR_AT:
            order.append((("lnvar",), None))
    for b in range(AB):
        order += [(("pT", 2 * b), None), (("pT", 2 * b + 1), None)]
        if b:
            order.append((("o", b - 1), None))
    order.append((("o", AB - 1), None))
    for n in range(CB):
        order += [(("conv", 2 * n), None), (("conv", 2 * n + 1), T_CONV + n)]
    for b in range(KB):
        for u in range(AB * b, AB * b + AB):
            if u % 8 == 7 and u != AB * b + AB - 1:
                order.append((None, T_ATT + u // 8))
        last = AB * b + AB - 1
        order.append((("attn", b), T_ATT + last // 8 if last % 8 == 7 else None))
    order += [(("mix", b), T_MIX + b) for b in range(KB)]
    order.append((("ssq2",), None))
    order += [(("wq", u), T_WQ + u) for u in range(HALVES)]
    return order


ORDER = jobs_in_order()
STEP_OF_JOB = {job: i + 1 for i, (job, _) in enumerate(ORDER) if job}
STEP_OF_TILE = {tile: i + 1 for i, (_, tile) in enumerate(ORDER) if tile is not None}
FRONT_STEPS = len(ORDER)
N_SC = 2 * HALVES // 4
JOBS = [job for job, _ in ORDER if job] + [("sc", j) for j in range(N_SC)]
_first_pT, _mix = JOBS.index(("pT", 0)), JOBS.index(("mix", 0))
BANK_OF = {job: i % 6 if i < _first_pT else (i - _first_pT) % 8 if i < _mix else 4 + (i - _mix + 2) % 4
           for i, job in enumerate(JOBS)}
BY_DVE = ("kb", "score", "lnsum", "o", "conv", "attn", "mix")


def freed_by_dve(job):
    return job[0] in BY_DVE or (job[0] in ("glu", "pT") and job[1] % 2 == 1)


FREED = {}
_n = {True: 0, False: 0}
for _job in JOBS:
    _n[freed_by_dve(_job)] += 1
    FREED[_job] = _n[freed_by_dve(_job)]

PAIRS = [(0, 2), (1, 3), (4, 6), (5, 7), (8, 10), (9, 11)]

C_N1, C_N2, C_GLU, C_DW, C_DWB = 0, 8, 16, 24, 24 + CB * TAPS
C_LNG = C_DWB + CB
C_LNB = C_LNG + CB
C_BP = C_LNB + CB
C_QG = C_BP + KB
C_KG = C_QG + 1
N_COLS = C_KG + 1


def hybrid_block(nc, x_t, front, cols, rel_bias, onehot, sub_keys, u_tiles, v_tiles, out):
    toeplitz = nc.dram_tensor("toeplitz", (HEADS, P * BW), F32, kind="Internal").ap()
    with ExitStack() as ctx:
        def sb(name, shape, dt=F32, stack=ctx):
            return stack.enter_context(nc.sbuf_tensor(name, shape, dt))

        def sem(name):
            return ctx.enter_context(nc.semaphore(name))

        bank = [ctx.enter_context(nc.psum_tensor(f"bank{i}", [P, 512], F32)) for i in range(8)]

        raw = sb("raw", [P, RING, D])
        hi = sb("hi", [P, RING, D], F32R)
        lo = sb("lo", [P, RING, D], F32R)
        nrm_hi = sb("nrm_hi", [P, KB, T], F32R)
        nrm_lo = sb("nrm_lo", [P, KB, T], F32R)
        ident = sb("ident", [P, P])
        iota = sb("iota", [P, TOPK])
        inner = ExitStack()

        def tmp(name, shape, dt=F32):
            return sb(name, shape, dt, inner)

        ones = tmp("ones", [P, P])
        prm = tmp("prm", [P, N_COLS])
        relx = tmp("relx", [BUCKETS + 1, HEADS])
        relb = tmp("relb", [BUCKETS + 1, HEADS, P])
        kmask = tmp("kmask", [P, 2 * HEADS - 2])
        ksel = tmp("ksel", [HEADS, AB, P])
        gains = tmp("gains", [P, 1])
        oneh = tmp("oneh", [BUCKETS + 1, GROUPS, BW])
        sq = tmp("sq", [P, KB, T])
        rs = tmp("rs", [P, 2, 512])
        u_pad = tmp("u_pad", [P, CB, TAPS - 1 + T])
        sig = tmp("sig", [P, CB, T])
        acc = tmp("acc", [P, CB, T])
        cu_hi = tmp("cu_hi", [P, CB, T], F32R)
        cu_lo = tmp("cu_lo", [P, CB, T], F32R)
        qk = tmp("qk", [P, 2 * AB, T])
        v = tmp("v", [P, TC, AW])
        gsig = tmp("gsig", [P, 2 * KB, T])
        bias = tmp("bias", [P, HEADS, T])
        prob = tmp("prob", [P, HEADS * BW])
        pT = tmp("pT", [P, 4, 3, P])
        o_hi = tmp("o_hi", [P, AB, T], F32R)
        o_lo = tmp("o_lo", [P, AB, T], F32R)
        stat = tmp("stat", [P, 16, TC * HEADS])
        resid = tmp("resid", [P, KB, T])
        inner.close()
        act = sb("act", [P, NK, T])
        iota_nk = sb("iota_nk", [P, NK, TOK], F16)
        keys = sb("keys", [P, 2, T], F16)
        parts = sb("parts", [P, 2, T], F16)
        ohA = sb("ohA", [P, 2, NK, TOK], F16)
        eqB = sb("eqB", [P, 2, HALF, TOK], F16)
        ohB = sb("ohB", [P, 2, 2, HALF, TOK], F16)

        p3 = prob[:, :].rearrange("p (h n) -> p h n", n=BW)
        qT = prob[:, 0:HALVES * T].rearrange("p (u t) -> p u t", t=T)
        skT = qk[:, 0:HALVES // 2, :].rearrange("p a t -> p (a t)").rearrange("p (u n) -> p u n", n=NK)
        negm, lsum, lnl, lse, ew, zz, fac = [stat[:, i, :] for i in range(7)]
        rq = stat[:, 9, :]
        rk = rs[0:HEADS, 1, 0:T]
        gmax, gsum = stat[:, 7, 0:TC * SLOTS], stat[:, 8, 0:TC * SLOTS]
        def part(t0, n):
            return act[:, t0:t0 + n, :].rearrange("p a t -> p (a t)")

        S = part(112, 16).rearrange("p (u n) -> p u n", n=NK)
        cand = part(104, 8).rearrange("p (h n) -> p h n", n=TOPK * TOPK)
        eq = part(96, 8)
        topv = part(64, 2).rearrange("p (u k) -> p u k", k=TOPK)
        topi = part(66, 2).bitcast(U32).rearrange("p (u k) -> p u k", k=TOPK)
        topf = part(68, 2).rearrange("p (u k) -> p u k", k=TOPK)
        bestv = part(70, 1).rearrange("p (u k) -> p u k", k=TOPK)
        besti = part(71, 1).bitcast(U32)
        bc1 = part(72, 1).bitcast(U32)
        bc2 = part(73, 1).bitcast(U32)
        cf1 = part(74, 1)
        cf2 = part(75, 1)
        sel = part(76, 2).rearrange("p (w c n) -> p w c n", w=2, c=TC)
        ex = part(78, 1)
        gate = part(79, 1).rearrange("p (c n) -> p c n", c=TC)
        pickf = part(81, 4).rearrange("p (a t) -> p a t", a=4)
        zs = part(80, 1)[:, 0:3 * TC * PH].rearrange("p (a n) -> p a n", a=3)
        yout = part(0, 8)

        raw_in = [sem(f"raw_in{i}") for i in range(RING)]
        x_in = [sem(f"x_in{i}") for i in range(2)]
        prm_in, rel_in, bias_out, bias_in, sk_in, y_out = [sem(s) for s in (
            "prm_in", "rel_in", "bias_out", "bias_in", "sk_in", "y_out")]
        hi_ready = sem("hi_ready")
        lo_ready = [sem(f"lo_ready{i}") for i in range(RING)]
        pe_step = sem("pe_step")
        act_evac, dve_evac = sem("act_evac"), sem("dve_evac")
        const = sem("const")
        squared = sem("squared")
        pair_sums = sem("pair_sums")
        normed = sem("normed")
        nhi, nlo = sem("nhi"), sem("nlo")
        relb_ready = sem("relb_ready")
        qk_sq = sem("qk_sq")
        gains_ready, rk_ready, rq_ready = sem("gains_ready"), sem("rk_ready"), sem("rq_ready")
        tap = sem("tap")
        score_max, exps, lns, wexp, scaled = sem("score_max"), sem("exps"), sem("lns"), sem("wexp"), sem("scaled")
        o_hi_ready = sem("o_hi_ready")
        centred, centred_sq, ln_out, silu, cu_h, cu_l, biased = [sem(s) for s in (
            "centred", "centred_sq", "ln_out", "silu", "cu_h", "cu_l", "biased")]
        gates_ready = sem("gates_ready")
        merged, m_hi, m_lo = sem("merged"), sem("m_hi"), sem("m_lo")
        chain = sem("chain")
        sc_ready = sem("sc_ready")
        gelu_done = sem("gelu_done")
        top_done, gexp, gate_ready, pick_T, pick_ready = [sem(s) for s in (
            "top_done", "gexp", "gate_ready", "pick_T", "pick_ready")]
        second, spread, gate_mm, gated = sem("second"), sem("spread"), sem("gate_mm"), sem("gated")
        a_hi, a_lo = sem("a_hi"), sem("a_lo")
        y_began, y_first = sem("y_began"), sem("y_first")
        y_dve, y_act = sem("y_dve"), sem("y_act")

        def wait(eng, s, value):
            if not isinstance(value, int) or value > 0:
                eng.wait_ge(s, value)

        def freed(eng, job):
            wait(eng, dve_evac if freed_by_dve(job) else act_evac, FREED[job])

        def job_done(eng, job):
            eng.wait_ge(pe_step, STEP_OF_JOB[job])

        def step_of(base, it, j):
            if isinstance(it, int) and base + 4 * it + j < N_FRONT:
                return STEP_OF_TILE[base + 4 * it + j]
            return it * 4 + (FRONT_STEPS + base + j - N_FRONT + 1)

        def slot_of(base, j):
            return (base + j) % RING

        def uses(base, it, j):
            return it + ((base + j) // RING + 1)

        def wait_raw(eng, base, it, j):
            eng.wait_ge(raw_in[slot_of(base, j)], uses(base, it, j) * 16)

        def split_hi(act_e, base, it, j):
            s = slot_of(base, j)
            wait_raw(act_e, base, it, j)
            if not (isinstance(it, int) and base + 4 * it + j < RING):
                wait(act_e, pe_step, step_of(base - 4, it, j))
            act_e.copy(hi[:, s, :], raw[:, s, :]).then_inc(hi_ready, 1)

        def by_dve(base, j):
            return slot_of(base, j) == 3 or (base + j >= G_SHARED and slot_of(base, j) == 1)

        def wait_lo(eng, base, it, j):
            eng.wait_ge(lo_ready[slot_of(base, j)], uses(base, it, j))

        def split_lo(eng, base, it, j):
            s = slot_of(base, j)
            eng.wait_ge(hi_ready, it * 4 + (base + j + 1))
            eng.tensor_tensor(lo[:, s, :], raw[:, s, :], hi[:, s, :].bitcast(F32), ALU.subtract)\
               .then_inc(lo_ready[s], 1)

        def copy_pT(eng, copy, h):
            job_done(eng, ("pT", h))
            if h >= 4:
                job_done(eng, ("o", (h - 4) // 2))
            copy(pT[:, h % 4, :, :], bank[BANK_OF[("pT", h)]][:, 0:3 * P].rearrange("p (a n) -> p a n", a=3))\
                .then_inc(dve_evac if freed_by_dve(("pT", h)) else act_evac, 1)

        U0, V0 = N_FRONT, N_FRONT + N_U
        S_U, S_V = FRONT_STEPS, FRONT_STEPS + N_U

        block = ctx.enter_context(nc.Block())

        @block.sync
        def _(sp):
            for r in range(2):
                sp.dma_start(resid[:, 4 * r:4 * r + 4, :], x_t[:, 4 * r:4 * r + 4, :]).then_inc(x_in[r], 16)
            sp.dma_start(oneh[:, :, :], onehot).then_inc(rel_in, 16)
            sp.dma_start(relx[0:BUCKETS, :], rel_bias).then_inc(rel_in, 16)
            sp.dma_start(prm[:, :], cols).then_inc(prm_in, 16)

            def load(src, base, it, j):
                if not (isinstance(it, int) and base + 4 * it + j < RING):
                    wait_lo(sp, base - 4, it, j)
                sp.dma_start(raw[:, slot_of(base, j), :], src).then_inc(raw_in[slot_of(base, j)], 16)

            for g in range(N_FRONT):
                load(front[g], g, 0, 0)
                if 5 <= g < 5 + HEADS // 2:
                    for h in (2 * (g - 5), 2 * (g - 5) + 1):
                        freed(sp, ("bias", h))
                        sp.dma_start(toeplitz[h].rearrange("(p w) -> p w", w=BW), p3[:, h, :]).then_inc(bias_out, 16)
                if g == 14:
                    sp.wait_ge(bias_out, 16 * HEADS)
                if 14 <= g < 14 + HEADS // 2:
                    for h in (2 * (g - 14), 2 * (g - 14) + 1):
                        sp.dma_start(bias[:, h, :], toeplitz[h, P - 1:P - 1 + P * (BW - 1)].rearrange(
                            "(p w) -> p w", w=BW - 1)[:, 0:T]).then_inc(bias_in, 16)
                if g == T_MIX:
                    freed(sp, ("score", 11))
                    sp.dma_start(skT, sub_keys).then_inc(sk_in, 16)
            with sp.Fori(0, N_U // RING) as it:
                for j in range(RING):
                    load(u_tiles[it * RING + j], U0, it, j)
            with sp.Fori(0, N_V // RING) as it:
                for j in range(RING):
                    load(v_tiles[it * RING + j], V0, it, j)
            for c in range(TC):
                sp.wait_ge(y_dve, c + 1)
                sp.wait_ge(y_act, c + 1)
                sp.dma_start(out[c], yout[:, c * D:(c + 1) * D]).then_inc(y_out, 16)
            sp.wait_ge(y_out, 16 * TC)

        @block.gpsimd
        def _(pool):
            pool.memset(relx[BUCKETS:BUCKETS + 1, :], NEG).then_inc(const, 1)
            pool.wait_ge(const, 1)
            pool.memset(ones[:, :], 1.0).then_inc(const, 1)
            pool.memset(ident[:, :], 0.0).then_inc(const, 1)
            pool.memset(u_pad[:, :, 0:TAPS - 1], 0.0).then_inc(const, 1)
            pool.memset(kmask[:, :], 0.0).then_inc(const, 1)
            pool.wait_ge(const, 5)
            for r in range(2):
                pool.memset(kmask[r * HD:(r + 1) * HD, HEADS - 2 + r:HEADS - 1 + r], 1.0).then_inc(const, 1)
                pool.wait_ge(const, 6 + r)
            pool.affine_select(out=ident[:, :], in_=ident[:, :], compare_op=ALU.not_equal, fill=1.0,
                               base=0, pattern=[[-1, P]], channel_multiplier=1).then_inc(const, 1)
            pool.iota(iota[:, :], pattern=[[1, TOPK]], base=0, channel_multiplier=0,
                      allow_small_or_imprecise_dtypes=True).then_inc(const, 1)

            def lo_of(g):
                if not by_dve(g, 0):
                    split_lo(pool, g, 0, 0)

            for g in range(N_FRONT + LEAD):
                lo_of(g)
            pool.wait_ge(y_began, 1)
            pool.wait_ge(normed, 2 * KB)
            pool.iota(iota_nk[:, :, :], pattern=[[1, NK], [0, TOK]], base=0, channel_multiplier=0,
                      allow_small_or_imprecise_dtypes=True).then_inc(const, 1)
            for base, tiles in ((U0 + LEAD, HALF), (G_SHARED, N_U + N_V - RING - HALF)):
                with pool.Fori(0, tiles // RING) as it:
                    for j in range(RING):
                        if not by_dve(base, j):
                            split_lo(pool, base, it, j)

        @block.scalar
        def _(a):
            def split_norm(k, round_):
                a.wait_ge(normed, KB * round_ + k + 1)
                a.copy(nrm_hi[:, k, :], sq[:, k, :]).then_inc(nhi, 1)

            def bias_rows(h):
                job_done(a, ("bias", h))
                a.copy(p3[:, h, :], bank[BANK_OF[("bias", h)]][:, 0:BW]).then_inc(act_evac, 1)

            a.preload_act_table(ACT.Sqrt)
            for r in range(2):
                a.wait_ge(x_in[r], 16)
                a.activation(sq[:, 4 * r:4 * r + 4, :], resid[:, 4 * r:4 * r + 4, :], ACT.Square)\
                 .then_inc(squared, 1)
            split_hi(a, 0, 0, 0)
            job_done(a, ("ssq1",))
            a.activation(rs[:, 0, 0:T], bank[BANK_OF[("ssq1",)]][:, 0:T], ACT.Sqrt, bias=EPS, scale=1.0 / D)\
             .then_inc(act_evac, 1)
            split_hi(a, 1, 0, 0)
            for h in range(3):
                bias_rows(h)
            for k in range(KB):
                split_norm(k, 0)
                if k < 4:
                    bias_rows(3 + k)
            split_hi(a, 2, 0, 0)

            def exp_of(s):
                c, pair = divmod(s, len(PAIRS))
                w = P * (c + 1)
                a.wait_ge(score_max, s + 1)
                for h in PAIRS[pair]:
                    pr = p3[:, h, c * P:c * P + w]
                    col = c * HEADS + h
                    a.activation(pr, pr, ACT.Exp, bias=negm[:, col:col + 1],
                                 accum_out=lsum[:, col:col + 1]).then_inc(exps, 1)

            def evac_front(n):
                if n < T_QK:
                    if n % 2 == 0:
                        b = n // 2
                        job_done(a, ("glu", n))
                        a.activation(sig[:, b, :], bank[BANK_OF[("glu", n)]][:, 0:T], ACT.Sigmoid,
                                     bias=prm[:, C_GLU + CB + b:C_GLU + CB + b + 1]).then_inc(act_evac, 1)
                elif n < T_V:
                    i = n - T_QK
                    job_done(a, ("qk", i))
                    b = bank[BANK_OF[("qk", i)]][:, 0:T]
                    if i == KB:
                        job_done(a, ("qss",))
                    elif i == 0:
                        a.wait_ge(nhi, KB)
                        a.wait_ge(nlo, KB)
                    a.activation(sq[:, i % KB, :], b, ACT.Square).then_inc(qk_sq, 1)
                    a.copy(qk[:, i, :], b).then_inc(act_evac, 1)
                elif n >= T_GATE:
                    i = n - T_GATE
                    job_done(a, ("gate", i))
                    a.copy(gsig[:, i, :], bank[BANK_OF[("gate", i)]][:, 0:T]).then_inc(act_evac, 1)
                if T_V <= n < T_GATE and (n - T_V) % 2:
                    i = (n - T_V) // 2
                    job_done(a, ("v", i))
                    a.copy(v[:, :, T * i:T * (i + 1)], bank[BANK_OF[("v", i)]][:, :].rearrange(
                        "p (c n) -> p c n", c=TC)).then_inc(act_evac, 1)
                for h in BIAS_AT.get(n, ()):
                    bias_rows(h)
                if n == QSS_AT:
                    job_done(a, ("qss",))
                    a.activation(rq[:, :], bank[BANK_OF[("qss",)]][:, 0:TC * HEADS], ACT.Sqrt, bias=HD * EPS)\
                     .then_inc(act_evac, 1)
                if n == KSS_AT:
                    job_done(a, ("kss",))
                    a.activation(rk, bank[BANK_OF[("kss",)]][0:HEADS, 0:T], ACT.Sqrt, bias=EPS, scale=1.0 / HD)\
                     .then_inc(act_evac, 1)

            for n in range(T_CONV):
                split_hi(a, n + LEAD, 0, 0)
                evac_front(n)
                for i in SCORES_AT.get(n - 2, ()):
                    exp_of(i)
                if n == WEIGHTS_AT:
                    a.wait_ge(exps, TC * HEADS)
                    a.activation(lnl[:, :], lsum[:, :], ACT.Ln).then_inc(lns, 1)
                if n == WEIGHTS_AT + 1:
                    a.wait_ge(wexp, TC)
                    a.activation(ew[:, :], lse[:, :], ACT.Exp).then_inc(lns, 1)
                if n == LNSUM_AT + 1:
                    job_done(a, ("kss",))
                    a.wait_ge(centred, 1)
                    a.activation(sq[:, 0:CB, :], u_pad[:, :, 0:T], ACT.Square).then_inc(centred_sq, 1)
                if n == LNVAR_AT:
                    job_done(a, ("lnvar",))
                    a.activation(rs[:, 0, 0:T], bank[BANK_OF[("lnvar",)]][:, 0:T], ACT.Sqrt, bias=EPS,
                                 scale=1.0 / CONV_CH).then_inc(act_evac, 1)
                    a.preload_act_table(ACT.Silu)

            def gate_sigmoid(i):
                freed(a, ("gate", 2 * KB - 1))
                a.activation(gsig[:, 4 * i:4 * i + 4, :], gsig[:, 4 * i:4 * i + 4, :], ACT.Sigmoid)\
                 .then_inc(gates_ready, 1)

            def copy_o(b):
                job_done(a, ("o", b))
                a.copy(o_hi[:, b, :], bank[BANK_OF[("o", b)]][:, 0:T]).then_inc(o_hi_ready, 1)

            for b in range(AB):
                copy_pT(a, a.copy, 2 * b)
                if b:
                    copy_o(b - 1)
                if b == 0:
                    a.wait_ge(ln_out, 1)
                if b in (0, 1):
                    for i in (2 * b, 2 * b + 1):
                        a.activation(acc[:, i, :], acc[:, i, :], ACT.Silu, bias=prm[:, C_LNB + i:C_LNB + i + 1],
                                     scale=prm[:, C_LNG + i:C_LNG + i + 1]).then_inc(silu, 1)
                if b == 2:
                    a.wait_ge(silu, CB)
                    a.copy(cu_hi[:, :, :], acc[:, :, :]).then_inc(cu_h, 1)
            copy_o(AB - 1)
            for n in range(T_CONV, T_ATT):
                gate_sigmoid(n - T_CONV)
                split_hi(a, n + LEAD, 0, 0)
            for b in range(KB):
                if T_ATT + b < T_MIX:
                    split_hi(a, T_ATT + b + LEAD, 0, 0)
                a.wait_ge(merged, b + 1)
                if b == 0:
                    job_done(a, ("gate", 2 * KB - 1))
                a.copy(nrm_hi[:, b, :], gsig[:, b, :]).then_inc(m_hi, 1)
            for b in range(KB):
                split_hi(a, T_MIX + b + LEAD, 0, 0)
                freed(a, ("mix", b))
                a.activation(sq[:, b, :], resid[:, b, :], ACT.Square).then_inc(squared, 1)
            job_done(a, ("ssq2",))
            a.activation(rs[:, 0, 0:T], bank[BANK_OF[("ssq2",)]][:, 0:T], ACT.Sqrt, bias=EPS, scale=1.0 / D)\
             .then_inc(act_evac, 1)
            for k in range(KB):
                split_norm(k, 1)
            for u in range(HALVES):
                split_hi(a, T_WQ + u + LEAD, 0, 0)
                job_done(a, ("wq", u))
                a.copy(qT[:, u, :], bank[BANK_OF[("wq", u)]][:, 0:T]).then_inc(act_evac, 1)
            for j in range(N_SC):
                a.wait_ge(sc_ready, j + 1)
                a.copy(S[:, 4 * j:4 * j + 4, :], bank[BANK_OF[("sc", j)]][:, :].rearrange(
                    "p (u n) -> p u n", n=NK)).then_inc(act_evac, 1)

            def gelu(base_i, it, j):
                a.wait_ge(pe_step, it * 4 + (S_U + base_i + j + 1))
                a.activation(act[:, it * 4 + (base_i + j), :], bank[4 + j % 2][:, 0:T], ACT.Gelu).then_inc(gelu_done, 1)

            a.preload_act_table(ACT.Gelu)
            with a.Fori(0, EXP_TILE // RING) as it:
                for j in range(RING):
                    split_hi(a, U0 + LEAD, it, j)
                    gelu(0, it, j)
            a.wait_ge(top_done, 1)
            a.activation(ex[:, :], ex[:, :], ACT.Exp).then_inc(gexp, 1)
            a.preload_act_table(ACT.Gelu)
            with a.Fori(EXP_TILE // RING, HALF // RING) as it:
                for j in range(RING):
                    split_hi(a, U0 + LEAD, it, j)
                    gelu(0, it, j)
            a.wait_ge(pick_ready, 2)
            with a.Fori(0, HALF // RING) as it:
                for j in range(RING):
                    split_hi(a, U0 + HALF + LEAD, it, j)
                    gelu(HALF, it, j)

            def a_split(base_i, it, j):
                wait(a, pe_step, it * 4 + (S_V + base_i + j - 3))
                a.copy(nrm_hi[:, (base_i + j) % RING, :], act[:, it * 4 + (base_i + j), :]).then_inc(a_hi, 1)

            a.wait_ge(pe_step, S_V)
            for half in range(2):
                a.wait_ge(gated, GROUPS_N * (half + 1))
                a_split(HALF * half, 0, 0)
                with a.Fori(0, HALF // RING - 1) as it:
                    for j in range(RING):
                        a_split(HALF * half + 1, it, j)
                        split_hi(a, V0 + HALF * half + LEAD, it, j)
                for j in range(RING):
                    if j < RING - 1:
                        a_split(HALF * (half + 1) - RING + 1, 0, j)
                    if half == 0 or j == 0:
                        split_hi(a, V0 + HALF * (half + 1) - RING + LEAD, 0, j)
            a.wait_ge(y_first, 1)
            a.copy(yout[:, 512:D], bank[1][:, :]).then_inc(y_act, 1)
            a.wait_ge(pe_step, S_V + N_V)
            a.copy(yout[:, D + 512:2 * D], bank[3][:, :]).then_inc(y_act, 1)

        @block.vector
        def _(dve):
            links = [0]

            def link(ins):
                links[0] += 1
                ins.then_inc(chain, 1)
                dve.wait_ge(chain, links[0])

            def lo_of(g):
                if by_dve(g, 0):
                    split_lo(dve, g, 0, 0)

            def normalise(gain, round_):
                def lower(k):
                    dve.wait_ge(nhi, KB * round_ + k + 1)
                    dve.tensor_tensor(nrm_lo[:, k, :], sq[:, k, :], nrm_hi[:, k, :].bitcast(F32), ALU.subtract)\
                       .then_inc(nlo, 1)

                link(dve.reciprocal(rs[:, 0, 0:T], rs[:, 0, 0:T]))
                for k in range(KB):
                    dve.scalar_tensor_tensor(out=sq[:, k, :], in0=resid[:, k, :], scalar=prm[:, gain + k:gain + k + 1],
                                             in1=rs[:, 0, 0:T], op0=ALU.mult, op1=ALU.mult).then_inc(normed, 1)
                    if k:
                        lower(k - 1)
                lower(KB - 1)

            for r in range(2):
                dve.wait_ge(squared, r + 1)
                dve.tensor_tensor(sq[:, 4 * r:4 * r + 2, :], sq[:, 4 * r:4 * r + 2, :], sq[:, 4 * r + 2:4 * r + 4, :],
                                  ALU.add).then_inc(pair_sums, 1)
                if r == 0:
                    dve.wait_ge(rel_in, 32)
                    dve.wait_ge(const, 1)
                    dve.tensor_copy(relb[:, :, :], relx[:, :].unsqueeze(2).broadcast_to([BUCKETS + 1, HEADS, P]))\
                       .then_inc(relb_ready, 1)
            dve.wait_ge(prm_in, 16)
            dve.tensor_tensor(gains[:, :], prm[:, C_QG:C_QG + 1], prm[:, C_KG:C_KG + 1], ALU.mult).then_inc(gains_ready, 1)
            freed(dve, ("ssq1",))
            normalise(C_N1, 0)
            for g in range(LEAD):
                lo_of(g)

            def glu(b):
                job_done(dve, ("glu", 2 * b + 1))
                freed(dve, ("glu", 2 * b))
                dve.scalar_tensor_tensor(out=u_pad[:, b, TAPS - 1:], in0=bank[BANK_OF[("glu", 2 * b + 1)]][:, 0:T],
                                         scalar=prm[:, C_GLU + b:C_GLU + b + 1], in1=sig[:, b, :],
                                         op0=ALU.add, op1=ALU.mult).then_inc(dve_evac, 1)

            def conv_tap(w):
                for b in range(CB):
                    src = u_pad[:, b, w:w + T]
                    wt = prm[:, C_DW + b * TAPS + w:C_DW + b * TAPS + w + 1]
                    part_sum = bank[6 + b // 2][:, (b % 2) * T:(b % 2 + 1) * T]
                    if w == 0:
                        dve.wait_ge(const, 4)
                        freed(dve, ("glu", 2 * b + 1))
                        dve.tensor_scalar(part_sum, src, wt, prm[:, C_DWB + b:C_DWB + b + 1], ALU.mult, ALU.add)\
                           .then_inc(tap, 1)
                    else:
                        dve.wait_ge(tap, CB * (w - 1) + b + 1)
                        dve.scalar_tensor_tensor(out=acc[:, b, :] if w == TAPS - 1 else part_sum, in0=src, scalar=wt,
                                                 in1=part_sum, op0=ALU.mult, op1=ALU.add).then_inc(tap, 1)

            def k_norm(i):
                two = qk[:, AB + 2 * i:AB + 2 * i + 2, :].rearrange("p a t -> p (a t)")
                job_done(dve, ("kb", i))
                if i == 0:
                    dve.wait_ge(gains_ready, 1)
                dve.scalar_tensor_tensor(out=two, in0=two, scalar=gains[:, 0:1], in1=bank[BANK_OF[("kb", i)]][:, :],
                                         op0=ALU.mult, op1=ALU.mult).then_inc(dve_evac, 1)

            def score(s):
                c, pair = divmod(s, len(PAIRS))
                h0 = PAIRS[pair][0]
                w = P * (c + 1)
                job_done(dve, ("score", s))
                for r, h in enumerate(PAIRS[pair]):
                    col = c * HEADS + h
                    ins = dve.scalar_tensor_tensor(out=p3[:, h, c * P:c * P + w],
                                                   in0=bank[BANK_OF[("score", s)]][:, r * w:(r + 1) * w],
                                                   scalar=rq[:, col:col + 1], in1=bias[:, h, T - w:T],
                                                   op0=ALU.mult, op1=ALU.add)
                    ins.then_inc(dve_evac if r else biased, 1)
                freed(dve, ("score", s))
                dve.wait_ge(biased, s + 1)
                dve.tensor_reduce(negm[:, c * HEADS + h0:c * HEADS + h0 + 3:2], p3[:, h0:h0 + 3:2, c * P:c * P + w],
                                  AX.X, ALU.max, negate=True).then_inc(score_max, 1)

            def group_weights():
                dve.wait_ge(lns, 1)
                link(dve.tensor_tensor(lse[:, :], lnl[:, :], negm[:, :], ALU.subtract))
                lse4 = lse[:, :].rearrange("p (c g s) -> p c s g", c=TC, g=GROUPS)
                for c in range(TC):
                    link(dve.tensor_reduce(gmax[:, c * SLOTS:(c + 1) * SLOTS], lse4[:, c], AX.X, ALU.max))
                for c in range(TC):
                    l3 = lse[:, c * HEADS:(c + 1) * HEADS].rearrange("p (g s) -> p g s", g=GROUPS)
                    m3 = gmax[:, c * SLOTS:(c + 1) * SLOTS].unsqueeze(1).broadcast_to([P, GROUPS, SLOTS])
                    dve.tensor_tensor(l3, l3, m3, ALU.subtract).then_inc(wexp, 1)

            def group_factors():
                dve.wait_ge(lns, 2)
                ew4 = ew[:, :].rearrange("p (c g s) -> p c s g", c=TC, g=GROUPS)
                for c in range(TC):
                    link(dve.tensor_reduce(gsum[:, c * SLOTS:(c + 1) * SLOTS], ew4[:, c], AX.X, ALU.add))
                for c in range(TC):
                    z3 = zz[:, c * HEADS:(c + 1) * HEADS].rearrange("p (g s) -> p g s", g=GROUPS)
                    l3 = lsum[:, c * HEADS:(c + 1) * HEADS].rearrange("p (g s) -> p g s", g=GROUPS)
                    g3 = gsum[:, c * SLOTS:(c + 1) * SLOTS].unsqueeze(1).broadcast_to([P, GROUPS, SLOTS])
                    link(dve.tensor_tensor(z3, l3, g3, ALU.mult))
                link(dve.reciprocal(fac[:, :], zz[:, :]))
                link(dve.tensor_tensor(fac[:, :], fac[:, :], ew[:, :], ALU.mult))

            def scale_probs(h):
                for c in range(TC):
                    pr = p3[:, h, c * P:(c + 1) * P + c * P]
                    col = c * HEADS + h
                    dve.tensor_scalar(pr, pr, fac[:, col:col + 1], None, ALU.mult).then_inc(scaled, 1)

            for n in range(T_CONV):
                lo_of(n + LEAD)
                if n < T_QK and n % 2:
                    glu(n // 2)
                for w_ in TAPS_AT.get(n, ()):
                    conv_tap(w_)
                if n == 3:
                    dve.wait_ge(const, 8)
                    dve.tensor_copy(ksel[:, :, :].rearrange("p b (r d) -> p b r d", r=2),
                                    ident[0:HEADS, 0:HEADS].rearrange("p (b r) -> p b r", r=2).unsqueeze(3)
                                    .broadcast_to([HEADS, AB, 2, HD])).then_inc(rk_ready, 1)
                if n == QSS_AT + 1:
                    freed(dve, ("qss",))
                    dve.reciprocal(rq[:, :], rq[:, :]).then_inc(rq_ready, 1)
                if n == KSS_AT + 1:
                    freed(dve, ("kss",))
                    dve.reciprocal(rk, rk).then_inc(rk_ready, 1)
                if n == KB_AT + 1:
                    for i in range(AB // 2):
                        k_norm(i)
                if n == min(SCORES_AT) + 1:
                    dve.wait_ge(bias_in, 16 * HEADS)
                    dve.wait_ge(rq_ready, 1)
                for i in SCORES_AT.get(n - 1, ()):
                    score(i)
                if n == WEIGHTS_AT + 1:
                    group_weights()
                if n == LNSUM_AT + 1:
                    job_done(dve, ("lnsum",))
                    dve.wait_ge(tap, CB * TAPS)
                    dve.tensor_scalar(rs[:, 1, 0:T], bank[BANK_OF[("lnsum",)]][:, 0:T], 1.0 / CONV_CH, None, ALU.mult)\
                       .then_inc(dve_evac, 1)
                    freed(dve, ("lnsum",))
                    dve.tensor_tensor(u_pad[:, :, 0:T], acc[:, :, :], rs[:, 1:2, 0:T].broadcast_to([P, CB, T]),
                                      ALU.subtract).then_inc(centred, 1)
                    group_factors()
                if n > LNSUM_AT + 1:
                    for h in range(4 * (n - LNSUM_AT - 2), min(8, 4 * (n - LNSUM_AT - 1))):
                        scale_probs(h)
            def low_o(b):
                dve.wait_ge(o_hi_ready, b + 1)
                dve.tensor_tensor(o_lo[:, b, :], bank[BANK_OF[("o", b)]][:, 0:T], o_hi[:, b, :].bitcast(F32),
                                  ALU.subtract).then_inc(dve_evac, 1)

            freed(dve, ("lnvar",))
            link(dve.reciprocal(rs[:, 0, 0:T], rs[:, 0, 0:T]))
            dve.tensor_tensor(acc[:, :, :], u_pad[:, :, 0:T], rs[:, 0:1, 0:T].broadcast_to([P, CB, T]), ALU.mult)\
               .then_inc(ln_out, 1)
            for b in range(AB):
                copy_pT(dve, dve.tensor_copy, 2 * b + 1)
                if b < 2:
                    scale_probs(8 + 2 * b)
                    scale_probs(9 + 2 * b)
                if b == 3:
                    dve.wait_ge(cu_h, 1)
                    dve.tensor_tensor(cu_lo[:, :, :], acc[:, :, :], cu_hi[:, :, :].bitcast(F32), ALU.subtract)\
                       .then_inc(cu_l, 1)
                if b:
                    low_o(b - 1)
            low_o(AB - 1)
            for b in range(KB):
                if b % 2 == 0:
                    lo_of(T_CONV + b // 2 + LEAD)
                job_done(dve, ("conv", b))
                dve.wait_ge(gates_ready, b // 4 + 1)
                dve.scalar_tensor_tensor(out=gsig[:, b, :], in0=bank[BANK_OF[("conv", b)]][:, 0:T],
                                         scalar=prm[:, C_BP + b:C_BP + b + 1], in1=gsig[:, b, :],
                                         op0=ALU.add, op1=ALU.mult).then_inc(dve_evac, 1)
            for b in range(KB):
                dve.wait_ge(gates_ready, 2 + b // 4 + 1)
                if T_ATT + b < T_MIX:
                    lo_of(T_ATT + b + LEAD)
                job_done(dve, ("attn", b))
                dve.tensor_tensor(gsig[:, KB + b, :], bank[BANK_OF[("attn", b)]][:, 0:T], gsig[:, KB + b, :],
                                  ALU.mult).then_inc(dve_evac, 1)
                freed(dve, ("attn", b))
                dve.tensor_tensor(gsig[:, b, :], gsig[:, b, :], gsig[:, KB + b, :], ALU.add).then_inc(merged, 1)
                dve.wait_ge(m_hi, b + 1)
                dve.wait_ge(merged, b + 1)
                dve.tensor_tensor(nrm_lo[:, b, :], gsig[:, b, :], nrm_hi[:, b, :].bitcast(F32), ALU.subtract)\
                   .then_inc(m_lo, 1)
            for b in range(KB):
                lo_of(T_MIX + b + LEAD)
                job_done(dve, ("mix", b))
                dve.tensor_tensor(resid[:, b, :], bank[BANK_OF[("mix", b)]][:, 0:T], resid[:, b, :], ALU.add)\
                   .then_inc(dve_evac, 1)
            freed(dve, ("ssq2",))
            dve.wait_ge(dve_evac, FREED[("mix", KB - 1)])
            normalise(C_N2, 1)
            for u in range(HALVES):
                lo_of(T_WQ + u + LEAD)

            dve.wait_ge(const, 9)

            def top16(pair):
                ended = [0, 0]
                for stage in range(5):
                    for r, (vals, idx, row) in enumerate(pair):
                        if stage:
                            dve.wait_ge(chain, ended[r])
                        if stage in (0, 3):
                            ins = dve.max(vals[:, 8 * (stage // 3):8 * (stage // 3) + 8], row)
                        elif stage == 2:
                            ins = dve.match_replace(row, vals[:, 0:8], row, LOWEST)
                        else:
                            f = 8 * (stage // 4)
                            ins = dve.max_index(idx[:, f:f + 8], vals[:, f:f + 8], row)
                        links[0] += 1
                        ended[r] = links[0]
                        ins.then_inc(chain, 1)
                dve.wait_ge(chain, links[0])

            def candidates(c):
                t3 = topv[:, c * HALVES:(c + 1) * HALVES, :]
                link(dve.tensor_tensor(cand[:, :, :].rearrange("p h (a b) -> p h a b", a=TOPK),
                                       t3[:, 0::2, :].unsqueeze(3).broadcast_to([P, PH, TOPK, TOPK]),
                                       t3[:, 1::2, :].unsqueeze(2).broadcast_to([P, PH, TOPK, TOPK]), ALU.add))

            def lookup(c, w, stage):
                pos = (cf1, cf2)[w][:, c * P:(c + 1) * P]
                e4 = eq[:, :].rearrange("p (h k j) -> p h k j", h=PH, k=TOPK)
                e3 = eq[:, :].rearrange("p (n j) -> p n j", j=TOPK)
                if stage == 0:
                    link(dve.tensor_tensor(e3, pos.unsqueeze(2).broadcast_to([P, PH * TOPK, TOPK]),
                                           iota[:, 0:TOPK].unsqueeze(1).broadcast_to([P, PH * TOPK, TOPK]),
                                           ALU.is_equal))
                elif stage == 1:
                    tf = topf[:, c * HALVES + w:(c + 1) * HALVES:2, :].unsqueeze(2).broadcast_to([P, PH, TOPK, TOPK])
                    link(dve.tensor_tensor(e4, e4, tf, ALU.mult))
                else:
                    link(dve.tensor_reduce(sel[:, w, c, :], e3, AX.X, ALU.add))

            def top_step(i):
                if i < HALVES:
                    if i % 2 == 0:
                        freed(dve, ("sc", i // 2))
                    top16([(topv[:, u, :], topi[:, u, :], S[:, u, :]) for u in (2 * i, 2 * i + 1)])
                elif i == HALVES:
                    link(dve.tensor_copy(topf[:, :, :], topi[:, :, :]))
                else:
                    c, r = divmod(i - HALVES - 1, CHUNK_STEPS)
                    both = slice(c * P, (c + 1) * P)
                    if r == 0:
                        candidates(c)
                    elif r <= PH // 2:
                        heads = (2 * r - 2, 2 * r - 1)
                        top16([(bestv[:, c * PH + h, :], besti[:, (c * PH + h) * TOPK:(c * PH + h + 1) * TOPK],
                                cand[:, h, :]) for h in heads])
                    elif r == PH // 2 + 1:
                        link(dve.tensor_scalar(bc1[:, both], besti[:, both], 4, None, ALU.logical_shift_right))
                        link(dve.tensor_scalar(bc2[:, both], besti[:, both], 15, None, ALU.bitwise_and))
                        link(dve.tensor_copy(cf1[:, both], bc1[:, both]))
                        link(dve.tensor_copy(cf2[:, both], bc2[:, both]))
                    elif r < PH // 2 + 8:
                        lookup(c, *divmod(r - PH // 2 - 2, 3))
                    else:
                        b3 = bestv[:, c * PH:(c + 1) * PH, :]
                        x3 = ex[:, both].rearrange("p (u k) -> p u k", k=TOPK)
                        ins = dve.tensor_tensor(x3, b3, b3[:, :, 0:1].broadcast_to([P, PH, TOPK]), ALU.subtract)
                        if c:
                            ins.then_inc(top_done, 1)
                        else:
                            link(ins)

            def softmax_gates():
                dve.wait_ge(gexp, 1)
                e3 = ex[:, :].rearrange("p (u k) -> p u k", k=TOPK)
                link(dve.tensor_reduce(zs[:, 0, :], e3, AX.X, ALU.add))
                link(dve.reciprocal(zs[:, 1, :], zs[:, 0, :]))
                dve.tensor_tensor(gate[:, :, :].rearrange("p c (u k) -> p (c u) k", k=TOPK), e3,
                                  zs[:, 1, :].unsqueeze(2).broadcast_to([P, TC * PH, TOPK]), ALU.mult)\
                   .then_inc(gate_ready, 1)

            weights = [21] * HALVES + [10] + TC * ([23] + [35] * (PH // 2) + [8] + [23] * 6 + [3])
            tile_of = [int(TOP_TILES * sum(weights[:n]) / sum(weights)) for n in range(len(weights))]
            for i in range(HALF):
                if by_dve(U0 + LEAD, i):
                    split_lo(dve, U0 + LEAD, 0, i)
                for n, tile in enumerate(tile_of):
                    if tile == i:
                        top_step(n)
                if i == EXP_TILE + 2:
                    softmax_gates()
            dve.wait_ge(pick_T, 1)
            dve.tensor_copy(keys[:, :, :], bank[6][:, :].rearrange("p (a t) -> p a t", a=2)).then_inc(pick_ready, 1)
            dve.wait_ge(pick_T, 2)
            link(dve.tensor_scalar(pickf[:, 0, :], bank[7][:, 0:T], GATE_SCALE, None, ALU.mult))
            link(dve.tensor_copy(parts[:, 0, :], pickf[:, 0, :]))
            dve.tensor_tensor(parts[:, 1, :], pickf[:, 0, :], parts[:, 0, :], ALU.subtract).then_inc(pick_ready, 1)
            dve.wait_ge(pick_ready, 2)
            dve.wait_ge(const, 10)

            def one_hots(half, it, g):
                n = it * 2 + (half * GROUPS_N + g)
                t = bass.ds(it * (2 * TOK) + g * TOK, TOK)
                wait(dve, gate_mm, n - 1)

                def at(x, m):
                    return x.unsqueeze(1).broadcast_to([P, m, TOK])

                dve.tensor_tensor(eqB[:, g % 2], iota_nk[:, half * HALF:(half + 1) * HALF, :], at(keys[:, 1, t], HALF),
                                  ALU.is_equal).then_inc(second, 1)
                dve.tensor_tensor(ohA[:, g % 2], iota_nk[:, :, :], at(keys[:, 0, t], NK), ALU.is_equal)\
                   .then_inc(spread, 1)
                dve.wait_ge(second, n + 1)
                dve.tensor_tensor(ohB[:, g % 2], eqB[:, g % 2].unsqueeze(1).broadcast_to([P, 2, HALF, TOK]),
                                  parts[:, :, t].unsqueeze(2).broadcast_to([P, 2, HALF, TOK]), ALU.mult)\
                   .then_inc(spread, 1)

            def multiply(half, it, g):
                n = it * 2 + (half * GROUPS_N + g)
                wait(dve, gate_mm, n + 1)
                av = act[:, half * HALF:(half + 1) * HALF, bass.ds(it * (2 * TOK) + g * TOK, TOK)]
                gv = bank[6 + g][:, 0:TOK * HALF].rearrange("p (q n) -> p n q", q=TOK)
                dve.scalar_tensor_tensor(out=av, in0=gv, scalar=1.0 / GATE_SCALE, in1=av, op0=ALU.mult, op1=ALU.mult)\
                   .then_inc(gated, 1)

            def low_part(base_i, it, j):
                dve.wait_ge(a_hi, it * 4 + (base_i + j + 1))
                s = (base_i + j) % RING
                dve.tensor_tensor(nrm_lo[:, s, :], act[:, it * 4 + (base_i + j), :], nrm_hi[:, s, :].bitcast(F32),
                                  ALU.subtract).then_inc(a_lo, 1)

            def gate_body(half, it, first=False, last=False):
                base = U0 + HALF if half == 0 else V0
                for j in range(RING):
                    if j == 0 and first:
                        dve.wait_ge(gelu_done, HALF * (half + 1))
                    if half == 1 and not (last and j == RING - 1):
                        low_part(1, it, j)
                    if j % 2 == 0:
                        multiply(half, it, j // 2)
                    elif not last:
                        one_hots(half, it, 2 + j // 2)
                    if by_dve(base + LEAD, j):
                        split_lo(dve, base + LEAD, it, j)

            for half in range(2):
                one_hots(half, 0, 0)
                one_hots(half, 0, 1)
                if half == 1:
                    low_part(0, 0, 0)
                gate_body(half, 0, first=True)
                with dve.Fori(1, HALF // RING - 1) as it:
                    gate_body(half, it)
                gate_body(half, HALF // RING - 1, last=True)
            low_part(HALF, 0, 0)
            with dve.Fori(0, HALF // RING - 1) as it:
                for j in range(RING):
                    low_part(HALF + 1, it, j)
                    if by_dve(V0 + HALF + LEAD, j):
                        split_lo(dve, V0 + HALF + LEAD, it, j)
            for j in range(RING - 1):
                low_part(N_V - RING + 1, 0, j)
                if j == 0:
                    split_lo(dve, V0 + N_V - 1, 0, 0)
            dve.wait_ge(y_first, 1)
            dve.tensor_copy(yout[:, 0:512], bank[0][:, :]).then_inc(y_dve, 1)
            dve.wait_ge(pe_step, S_V + N_V)
            dve.tensor_copy(yout[:, D:D + 512], bank[2][:, :]).then_inc(y_dve, 1)

        @block.tensor
        def _(pe):
            done = [0]

            def step(ins):
                done[0] += 1
                ins.then_inc(pe_step, 1)

            def start(job):
                before = [other for other in JOBS[:JOBS.index(job)] if BANK_OF[other] == BANK_OF[job]]
                if before:
                    freed(pe, before[-1])
                return bank[BANK_OF[job]]

            def product(dst, s, units, vec_hi, vec_lo, base, it, j, first=True, last=True):
                wait_lo(pe, base, it, j)
                n = len(units)
                for i, (u, k) in enumerate(units):
                    for p_, (w_, x_) in enumerate(((hi, vec_hi), (hi, vec_lo), (lo, vec_hi))):
                        ins = pe.matmul(dst, w_[:, s, u * P:(u + 1) * P], x_[:, k, :],
                                        start=first and i == 0 and p_ == 0, stop=last and i == n - 1 and p_ == 2)
                return ins

            def full(n, job):
                b = start(job)
                return product(b[:, 0:T], n % RING, [(k, k) for k in range(KB)], nrm_hi, nrm_lo, n, 0, 0)

            def bias_row(h):
                b = start(("bias", h))
                step(pe.matmul(b[:, 0:BW], relb[:, h, :], oneh[:, h // SLOTS, :], start=True, stop=True))

            pe.wait_ge(const, 2)
            for _ in range(WARM_UP):
                pe.matmul(bank[5][:, 0:P], ones[:, :], ones[:, :], start=True, stop=True)
            pe.wait_ge(const, 7)
            b = start(("ssq1",))
            for k in range(4):
                pe.wait_ge(pair_sums, k // 2 + 1)
                ins = pe.matmul(b[:, 0:T], ones[:, :], sq[:, 4 * (k // 2) + k % 2, :], start=k == 0, stop=k == 3)
            step(ins)
            pe.wait_ge(relb_ready, 1)
            pe.wait_ge(rel_in, 32)
            for h in range(7):
                bias_row(h)

            def two_tiles(jobs, tiles, parts_ready):
                banks = [start(job) for job in jobs]
                for k in range(KB):
                    parts_ready(k)
                    for b, n in zip(banks, tiles):
                        ins = product(b[:, 0:T], n % RING, [(k, k)], nrm_hi, nrm_lo, n, 0, 0,
                                      first=k == 0, last=k == KB - 1)
                        if k == KB - 1:
                            step(ins)

            def norm_ready(round_):
                def wait_k(k):
                    pe.wait_ge(nlo, KB * round_ + k + 1)
                return wait_k

            def q_sums():
                b = start(("qss",))
                pe.wait_ge(qk_sq, AB)
                for c in range(TC):
                    for i in range(AB):
                        col = c * HEADS + 2 * i
                        ins = pe.matmul(b[:, col:col + 2], sq[:, i, c * P:(c + 1) * P], kmask[:, HEADS - 2:HEADS],
                                        start=c == 0 and i == 0, stop=True, skip_group_check=True)
                step(ins)

            def k_sums():
                b = start(("kss",))
                pe.wait_ge(qk_sq, 2 * AB)
                for i in range(AB):
                    ins = pe.matmul(b[0:HEADS, 0:T], kmask[:, HEADS - 2 - 2 * i:2 * HEADS - 2 - 2 * i],
                                    sq[:, (AB + i) % KB, :], start=i == 0, stop=i == AB - 1)
                step(ins)

            def spread_k(i):
                b = start(("kb", i))
                pe.wait_ge(rk_ready, 2)
                for r in range(2):
                    ins = pe.matmul(b[:, r * T:(r + 1) * T], ksel[:, 2 * i + r, :], rk,
                                    start=r == 0, stop=True, skip_group_check=True)
                step(ins)

            def v_tile_of(n):
                i, r = divmod(n - T_V, 2)
                b = start(("v", i)) if r == 0 else bank[BANK_OF[("v", i)]]
                wait_lo(pe, n, 0, 0)
                for m in range(KB // 2):
                    k = r * (KB // 2) + m
                    for c in range(TC):
                        for w_, x_ in ((hi, nrm_hi), (lo, nrm_hi), (hi, nrm_lo)):
                            ins = pe.matmul(b[:, c * T:(c + 1) * T], x_[:, k, c * P:(c + 1) * P],
                                            w_[:, n % RING, 2 * m * P:2 * (m + 1) * P],
                                            start=k == 0 and c == 0 and w_ is hi and x_ is nrm_hi,
                                            stop=k == KB - 1 and x_ is nrm_lo, skip_group_check=True)
                step(ins)

            def scores(s):
                c, pair = divmod(s, len(PAIRS))
                w = P * (c + 1)
                b = start(("score", s))
                freed(pe, ("kb", AB // 2 - 1))
                for r, h in enumerate(PAIRS[pair]):
                    rows = slice((h % 2) * HD, (h % 2 + 1) * HD)
                    ins = pe.matmul(b[:, r * w:(r + 1) * w], qk[rows, h // 2, c * P:(c + 1) * P],
                                    qk[rows, AB + h // 2, 0:w], start=r == 0, stop=True, skip_group_check=True)
                step(ins)

            for n in range(T_CONV):
                if n == 0:
                    two_tiles([("glu", 0), ("glu", 1)], [0, 1], norm_ready(0))
                elif n == 1:
                    pass
                elif n < T_QK:
                    step(full(n, ("glu", n)))
                elif n < T_V:
                    step(full(n, ("qk", n - T_QK)))
                elif n < T_GATE:
                    v_tile_of(n)
                else:
                    step(full(n, ("gate", n - T_GATE)))
                for h in BIAS_AT.get(n, ()):
                    bias_row(h)
                if n == QSS_AT:
                    q_sums()
                if n == KSS_AT:
                    k_sums()
                if n == KB_AT:
                    for i in range(AB // 2):
                        spread_k(i)
                for i in SCORES_AT.get(n, ()):
                    scores(i)
                if n == LNSUM_AT:
                    b = start(("lnsum",))
                    pe.wait_ge(tap, CB * TAPS)
                    for k in range(CB):
                        ins = pe.matmul(b[:, 0:T], ones[:, :], acc[:, k, :], start=k == 0, stop=k == CB - 1)
                    step(ins)
                if n == LNVAR_AT:
                    b = start(("lnvar",))
                    pe.wait_ge(centred_sq, 1)
                    for k in range(CB):
                        ins = pe.matmul(b[:, 0:T], ones[:, :], sq[:, k, :], start=k == 0, stop=k == CB - 1)
                    step(ins)

            def turn(h):
                b = start(("pT", h))
                pe.wait_ge(scaled, 2 * h + 2)
                pe.wait_ge(const, 8)
                for r in range(3):
                    ins = pe.transpose(b[:, r * P:(r + 1) * P], p3[:, h, r * P:(r + 1) * P], ident[:, :])
                step(ins)

            freed(pe, ("v", AB // 2 - 1))

            def attend(bl):
                b = start(("o", bl))
                for r in range(2):
                    h = 2 * bl + r
                    freed(pe, ("pT", h))
                    dst = b[r * HD:(r + 1) * HD, 0:T]
                    vv = [v[:, c, h * HD:(h + 1) * HD] for c in range(TC)]
                    pe.matmul(dst[:, 0:P], vv[0], pT[:, h % 4, 0, :], start=True, stop=True, skip_group_check=True)
                    pe.matmul(dst[:, P:T], vv[0], pT[:, h % 4, 1, :], start=True, stop=False, skip_group_check=True)
                    ins = pe.matmul(dst[:, P:T], vv[1], pT[:, h % 4, 2, :], start=False, stop=True,
                                    skip_group_check=True)
                step(ins)

            for bl in range(AB):
                turn(2 * bl)
                turn(2 * bl + 1)
                if bl:
                    attend(bl - 1)
            attend(AB - 1)
            pe.wait_ge(cu_l, 1)
            for b_ in range(KB):
                n = T_CONV + b_ // 2
                b = start(("conv", b_))
                step(product(b[:, 0:T], n % RING, [((b_ % 2) * CB + k, k) for k in range(CB)], cu_hi, cu_lo, n, 0, 0))
            freed(pe, ("o", AB - 1))
            for b_ in range(KB):
                b = start(("attn", b_))
                units = list(range(AB * b_, AB * b_ + AB))
                for tile in sorted({u // 8 for u in units}):
                    mine = [u for u in units if u // 8 == tile]
                    n = T_ATT + tile
                    ins = product(b[:, 0:T], n % RING, [(u % 8, u % AB) for u in mine], o_hi, o_lo, n, 0, 0,
                                  first=mine[0] == units[0], last=mine[-1] == units[-1])
                    if mine[-1] == units[-1] or mine[-1] % 8 == 7:
                        step(ins)
            two_tiles([("mix", 0), ("mix", 1)], [T_MIX, T_MIX + 1], lambda k: pe.wait_ge(m_lo, k + 1))
            for b_ in range(2, KB):
                step(full(T_MIX + b_, ("mix", b_)))
            b = start(("ssq2",))
            for k in range(KB):
                pe.wait_ge(squared, 2 + k + 1)
                ins = pe.matmul(b[:, 0:T], ones[:, :], sq[:, k, :], start=k == 0, stop=k == KB - 1)
            step(ins)
            freed(pe, ("attn", KB - 1))
            freed(pe, ("mix", KB - 1))
            for c in range(TC):
                for k in range(KB):
                    ins = pe.matmul(bank[2 * c + k // 4][:, (k % 4) * P:(k % 4 + 1) * P], resid[:, k, c * P:(c + 1) * P],
                                    ident[:, :], start=k % 4 == 0, stop=False, skip_group_check=True)
            ins.then_inc(y_began, 1)
            two_tiles([("wq", 0), ("wq", 1)], [T_WQ, T_WQ + 1], norm_ready(1))
            for u in range(2, HALVES):
                step(full(T_WQ + u, ("wq", u)))
            assert done[0] == FRONT_STEPS
            pe.wait_ge(sk_in, 16)
            for j in range(N_SC):
                b = start(("sc", j))
                for r in range(4):
                    c, u = divmod(4 * j + r, HALVES)
                    freed(pe, ("wq", u))
                    ins = pe.matmul(b[:, r * NK:(r + 1) * NK], qT[:, u, c * P:(c + 1) * P], skT[:, u, :],
                                    start=r == 0, stop=True, skip_group_check=True)
                ins.then_inc(sc_ready, 1)
            for job in JOBS[-4:]:
                if BANK_OF[job] < 6:
                    freed(pe, job)

            def u_tile(base_i, it, j):
                wait(pe, gelu_done, it * 4 + (base_i + j - 1))
                ins = product(bank[4 + j % 2][:, 0:T], j, [(k, k) for k in range(KB)], nrm_hi, nrm_lo, U0 + base_i, it, j)
                ins.then_inc(pe_step, 1)

            def gates(half, it):
                for g in range(2):
                    n = it * 2 + (half * GROUPS_N + g)
                    pe.wait_ge(spread, n * 2 + 2)
                    for q in range(TOK):
                        for i in range(2):
                            ins = pe.matmul(bank[6 + g][:, q * HALF:(q + 1) * HALF], ohA[:, g, :, q],
                                            ohB[:, g, i, :, q], start=i == 0, stop=i == 1, skip_group_check=True)
                    ins.then_inc(gate_mm, 1)

            for j in range(RING):
                u_tile(0, 0, j)
            with pe.Fori(1, PICK_TILE // RING) as it:
                for j in range(RING):
                    u_tile(0, it, j)
            freed(pe, ("sc", N_SC - 1))
            pe.wait_ge(top_done, 1)
            for w in range(2):
                for c in range(TC):
                    ins = pe.transpose(bank[6][:, w * T + c * P:w * T + (c + 1) * P], sel[:, w, c, :], ident[:, :])
            ins.then_inc(pick_T, 1)
            pe.wait_ge(gate_ready, 1)
            for c in range(TC):
                ins = pe.transpose(bank[7][:, c * P:(c + 1) * P], gate[:, c, :], ident[:, :])
            ins.then_inc(pick_T, 1)
            with pe.Fori(PICK_TILE // RING, HALF // RING) as it:
                for j in range(RING):
                    u_tile(0, it, j)

            def u_and_gates(it):
                gates(0, it)
                for j in range(RING):
                    u_tile(HALF, it, j)

            u_and_gates(0)
            with pe.Fori(1, HALF // RING) as it:
                u_and_gates(it)

            def v_tile(base_i, it, j, stop=False):
                wait_lo(pe, V0 + base_i, it, j)
                pe.wait_ge(a_hi, it * 4 + (base_i + j + 1))
                for c in range(TC):
                    for a_, v_ in ((nrm_hi, hi), (nrm_hi, lo), (nrm_lo, hi)):
                        if c == 0 and a_ is nrm_lo:
                            pe.wait_ge(a_lo, it * 4 + (base_i + j + 1))
                        for half in range(2):
                            ins = pe.matmul(bank[2 * c + half][:, :], a_[:, j, c * P:(c + 1) * P],
                                            v_[:, j, half * 512:(half + 1) * 512],
                                            start=False, stop=stop and a_ is nrm_lo, skip_group_check=True)
                    if stop and c == 0:
                        ins.then_inc(y_first, 1)
                ins.then_inc(pe_step, 1)

            def v_and_gates(it):
                gates(1, it)
                for j in range(RING):
                    v_tile(0, it, j)

            v_and_gates(0)
            with pe.Fori(1, HALF // RING) as it:
                v_and_gates(it)
            with pe.Fori(0, HALF // RING - 1) as it:
                for j in range(RING):
                    v_tile(HALF, it, j)
            for j in range(RING):
                v_tile(N_V - RING, 0, j, stop=j == RING - 1)


def bucket_rows():
    n = 255 - np.arange(BW)
    exact = BUCKETS // 2
    nf = np.maximum(n, 1).astype(np.float32)
    large = exact + (np.log(nf / np.float32(exact)) / np.float32(np.log(MAX_DISTANCE / exact))
                     * np.float32(BUCKETS - exact)).astype(np.int32)
    bucket = np.where(n < exact, n, np.minimum(large, BUCKETS - 1))
    rows = np.zeros((BUCKETS + 1, GROUPS, BW), np.float32)
    for g, (window, dilation) in enumerate(WINDOWS):
        valid = (n >= 0) & (n <= window) & (n % dilation == 0)
        rows[np.where(valid, bucket, BUCKETS), g, np.arange(BW)] = 1.0
    return rows


def kernel(**inputs):
    from concourse.bacc import Bacc
    from concourse.bass_utils import run_bass_kernel_spmd

    a = {k: np.asarray(x) for k, x in inputs.items()}

    def tiles(w, blocks):
        k = w.shape[0] // P
        return w.reshape(k, P, -1, P).transpose(2, 0, 1, 3)[blocks].reshape(-1, 8, P, P)\
                .transpose(0, 2, 1, 3).reshape(-1, P, 8 * P)

    glu = [b for pair in zip(range(CB, 2 * CB), range(CB)) for b in pair]
    n_in = a["w_in"].shape[2] // P
    n_v = 2 * CB + 2 * AB
    w_v = a["w_in"][0][:, n_v * P:(n_v + AB) * P].reshape(KB, P, AB // 2, 2, P).transpose(2, 0, 3, 1, 4)\
        .reshape(-1, 8, P, P).transpose(0, 2, 1, 3).reshape(-1, P, 8 * P)
    front = np.concatenate([
        tiles(a["w_in"][0], glu + list(range(2 * CB, n_v))),
        w_v,
        tiles(a["w_in"][0], list(range(n_v + AB, n_in))),
        tiles(a["conv_w_proj"][0], list(range(KB))),
        tiles(a["attn_w_proj"][0], list(range(KB))),
        tiles(a["mix_w_out"][0], list(range(KB))),
        tiles(a["peer_w_q"][0], list(range(HALVES))),
    ])

    def col(x):
        return x.reshape(-1, P).T

    cols = np.concatenate([
        col(a["norm1_g"][0]), col(a["norm2_g"][0]), col(a["conv_b_glu"][0]),
        a["conv_dw_w"][0, :, 0].reshape(TAPS, CB, P).transpose(2, 1, 0).reshape(P, CB * TAPS),
        col(a["conv_dw_b"][0]), col(a["conv_ln_g"][0]), col(a["conv_ln_b"][0]), col(a["conv_b_proj"][0]),
        np.tile(a["q_norm_g"][0], 2)[:, None], np.tile(a["k_norm_g"][0], 2)[:, None],
    ], axis=1)
    arrays = {
        "x_t": a["x"][0].T.reshape(KB, P, T).transpose(1, 0, 2),
        "front": front,
        "cols": cols,
        "rel_bias": a["rel_bias"],
        "onehot": bucket_rows(),
        "sub_keys": a["peer_sub_keys"][0].reshape(HALVES, NK, P).transpose(2, 0, 1),
        "u_tiles": a["peer_u"][0].reshape(NK, NK, KB, P).transpose(1, 3, 2, 0).reshape(NK, P, D),
        "v_tiles": a["peer_v"][0].reshape(NK, NK, D).transpose(1, 0, 2),
    }
    arrays = {k: np.ascontiguousarray(x) for k, x in arrays.items()}
    nc = Bacc("TRN2", target_bir_lowering=False, num_devices=1)
    args = [nc.dram_tensor(k, x.shape, mybir.dt.from_np(x.dtype), kind="ExternalInput").ap()
            for k, x in arrays.items()]
    y = nc.dram_tensor("y", (TC, P, D), F32, kind="ExternalOutput").ap()
    hybrid_block(nc, *args, y)
    r = run_bass_kernel_spmd(nc, [arrays], core_ids=[0])
    return r.results[0]["y"].reshape(1, T, D)
```
